# Optimizing a Trainium2 kernel written in Bass

```python
import jax, jax.numpy as jnp
from jax import lax
import numpy as np

D_MODEL = 2048
BATCH = 1
SEQ = 512
DEPTH = 1
DEC_BATCH = 8
DEC_SEQ = 8
PAST_LEN = 4096
PAGE_SIZE = 128

D_MIX = D_MODEL
HEAD_DIM = 128
A_WIDTH = D_MIX // 2
A_HEADS = A_WIDTH // HEAD_DIM
B_WIDTH = D_MIX - A_WIDTH
B_GROUPS = B_WIDTH // HEAD_DIM
CHUNK = 128
CONV_W = 3
D_FF = ((8 * D_MODEL) // 3 + 255) // 256 * 256
IN_COLS = 2 * A_WIDTH + 3 * B_WIDTH
EPS = 1e-6

kernel_name = "hybrid_chunk_sgu_shortconv_convffn_step"

def rmsnorm(x, g):
    xf = x.astype(jnp.float32)
    xf = xf * lax.rsqrt(jnp.mean(xf * xf, axis=-1, keepdims=True) + EPS)
    return (xf * g.astype(jnp.float32)).astype(x.dtype)

def group_rmsnorm(y, g, n_groups):
    shp = y.shape
    yf = y.astype(jnp.float32).reshape(shp[:-1] + (n_groups, shp[-1] // n_groups))
    yf = yf * lax.rsqrt(jnp.mean(yf * yf, axis=-1, keepdims=True) + EPS)
    return (yf.reshape(shp) * g.astype(jnp.float32)).astype(y.dtype)

def causal_dwconv(z, prev, w, b):
    T = z.shape[1]
    zc = jnp.concatenate([prev.astype(z.dtype), z], axis=1)
    out = b.astype(z.dtype) + sum(w[k].astype(z.dtype) * zc[:, k:k + T] for k in range(CONV_W))
    return out, zc[:, T:]

def chunk_sgu(v, w_s, b_s):
    Bn, T, _ = v.shape
    L = min(T, CHUNK)
    n = -(-T // CHUNK)
    pad = n * L - T
    vp = jnp.pad(v, ((0, 0), (0, pad), (0, 0)))
    vr = vp.reshape(Bn, n, L, A_HEADS, HEAD_DIM)
    mask = jnp.tril(jnp.ones((L, L), dtype=bool))
    ws = w_s[:, :L, :L]
    ws = jnp.where(mask[None], ws, jnp.zeros_like(ws)).astype(v.dtype)
    bias = b_s[:, :L].T.astype(v.dtype)[None, None, :, :, None]
    mixed = jnp.einsum('hij,bcjhd->bcihd', ws, vr) + bias
    return mixed.reshape(Bn, n * L, A_WIDTH)[:, :T]

def layer(x, mix_prev, ffn_prev, norm_mix_g, w_in, sgu_norm_g, w_s, b_s,
          conv_mix_w, conv_mix_b, out_norm_a_g, out_norm_b_g, w_out,
          norm_ffn_g, w_gate, w_up, conv_ffn_w, conv_ffn_b, w_down):
    h = rmsnorm(x, norm_mix_g)
    p = h @ w_in
    o1, o2, o3, o4 = A_WIDTH, 2 * A_WIDTH, 2 * A_WIDTH + B_WIDTH, 2 * A_WIDTH + 2 * B_WIDTH
    u = jax.nn.gelu(p[..., :o1])
    v = rmsnorm(jax.nn.gelu(p[..., o1:o2]), sgu_norm_g)
    bg, cg, xb = p[..., o2:o3], p[..., o3:o4], p[..., o4:]
    y_a = u * chunk_sgu(v, w_s, b_s)
    zc, new_mix = causal_dwconv(cg * xb, mix_prev, conv_mix_w, conv_mix_b)
    y_b = bg * zc
    y = jnp.concatenate([group_rmsnorm(y_a, out_norm_a_g, A_HEADS),
                         group_rmsnorm(y_b, out_norm_b_g, B_GROUPS)], axis=-1)
    x = x + y @ w_out
    h = rmsnorm(x, norm_ffn_g)
    gate, new_ffn = causal_dwconv(h @ w_gate, ffn_prev, conv_ffn_w, conv_ffn_b)
    x = x + (jax.nn.silu(gate) * (h @ w_up)) @ w_down
    return x, new_mix, new_ffn, v

def setup_inputs(seed: int = 0) -> dict:
    key = jax.random.key(seed)
    ks = jax.random.split(key, 24)
    f32 = jnp.float32
    nrm = lambda k, s, sc=1.0: (jax.random.normal(k, s, f32) * sc)
    gain = lambda k, s: 1.0 + 0.1 * jax.random.normal(k, s, f32)
    return {
        "x_prompt": nrm(ks[0], (BATCH, SEQ, D_MODEL)),
        "x_sample": nrm(ks[1], (DEC_BATCH, DEC_SEQ, D_MODEL)),
        "state_conv_mix": nrm(ks[2], (DEPTH, DEC_BATCH, CONV_W - 1, B_WIDTH)),
        "state_conv_ffn": nrm(ks[3], (DEPTH, DEC_BATCH, CONV_W - 1, D_FF)),
        "norm_mix_g": gain(ks[4], (DEPTH, D_MODEL)),
        "w_in": nrm(ks[5], (DEPTH, D_MODEL, IN_COLS), D_MODEL ** -0.5),
        "sgu_norm_g": gain(ks[6], (DEPTH, A_WIDTH)),
        "w_s": nrm(ks[7], (DEPTH, A_HEADS, CHUNK, CHUNK), CHUNK ** -0.5),
        "b_s": gain(ks[8], (DEPTH, A_HEADS, CHUNK)),
        "conv_mix_w": nrm(ks[9], (DEPTH, CONV_W, B_WIDTH), CONV_W ** -0.5),
        "conv_mix_b": nrm(ks[10], (DEPTH, B_WIDTH), 0.01),
        "out_norm_a_g": gain(ks[11], (DEPTH, A_WIDTH)),
        "out_norm_b_g": gain(ks[12], (DEPTH, B_WIDTH)),
        "w_out": nrm(ks[13], (DEPTH, D_MIX, D_MODEL), D_MIX ** -0.5),
        "norm_ffn_g": gain(ks[14], (DEPTH, D_MODEL)),
        "w_gate": nrm(ks[15], (DEPTH, D_MODEL, D_FF), D_MODEL ** -0.5),
        "w_up": nrm(ks[16], (DEPTH, D_MODEL, D_FF), D_MODEL ** -0.5),
        "conv_ffn_w": nrm(ks[17], (DEPTH, CONV_W, D_FF), CONV_W ** -0.5),
        "conv_ffn_b": nrm(ks[18], (DEPTH, D_FF), 0.01),
        "w_down": nrm(ks[19], (DEPTH, D_FF, D_MODEL), D_FF ** -0.5),
        "final_norm_g": gain(ks[20], (D_MODEL,)),
    }

def reference(x_prompt, x_sample, state_conv_mix, state_conv_ffn,
              norm_mix_g, w_in, sgu_norm_g, w_s, b_s, conv_mix_w, conv_mix_b,
              out_norm_a_g, out_norm_b_g, w_out, norm_ffn_g, w_gate, w_up,
              conv_ffn_w, conv_ffn_b, w_down, final_norm_g):
    xp, xs = x_prompt, x_sample
    mix_p, ffn_p, mix_s, ffn_s, v_s = [], [], [], [], []
    for l in range(DEPTH):
        params = (norm_mix_g[l], w_in[l], sgu_norm_g[l], w_s[l], b_s[l],
                  conv_mix_w[l], conv_mix_b[l], out_norm_a_g[l], out_norm_b_g[l], w_out[l],
                  norm_ffn_g[l], w_gate[l], w_up[l], conv_ffn_w[l], conv_ffn_b[l], w_down[l])
        zero_mix = jnp.zeros((xp.shape[0], CONV_W - 1, B_WIDTH), xp.dtype)
        zero_ffn = jnp.zeros((xp.shape[0], CONV_W - 1, D_FF), xp.dtype)
        xp, nm, nf, _ = layer(xp, zero_mix, zero_ffn, *params)
        mix_p.append(nm)
        ffn_p.append(nf)
        xs, nm, nf, vrows = layer(xs, state_conv_mix[l], state_conv_ffn[l], *params)
        mix_s.append(nm)
        ffn_s.append(nf)
        v_s.append(vrows)
    y_prompt = rmsnorm(xp, final_norm_g)
    y_sample = rmsnorm(xs, final_norm_g)
    new_conv_mix_prompt = jnp.stack(mix_p)
    new_conv_ffn_prompt = jnp.stack(ffn_p)
    new_conv_mix_sample = jnp.stack(mix_s)
    new_conv_ffn_sample = jnp.stack(ffn_s)
    new_chunk_v_sample = jnp.stack(v_s)
    return (y_prompt, y_sample, new_conv_mix_prompt, new_conv_ffn_prompt,
            new_conv_mix_sample, new_conv_ffn_sample, new_chunk_v_sample)


_drawn_inputs = setup_inputs


def setup_inputs(seed=0):
    import zlib

    import numpy as np

    out = dict(_drawn_inputs(seed))
    spreads = {}
    factors = {'conv_mix_b': 8.0, 'conv_ffn_b': 8.0}
    for name, (base, spread) in spreads.items():
        noise = np.random.default_rng([zlib.crc32(name.encode()), seed]).standard_normal(out[name].shape)
        drawn = base * np.exp(spread * noise) if base else spread * noise
        out[name] = __import__('jax').numpy.asarray(drawn.astype(out[name].dtype))
    for name, factor in factors.items():
        out[name] = (out[name] * factor).astype(out[name].dtype)
    return out
```

```python
from contextlib import ExitStack

import concourse.bass as bass
from concourse import mybir

F32 = mybir.dt.float32
F32R = mybir.dt.float32r
ALU = mybir.AluOpType
ACT = mybir.ActivationFunctionType
ds = bass.ds

P = 128


def build_layer(nc, x_prompt, x_sample, state_conv_mix, state_conv_ffn, norm_mix_g, w_in, sgu_norm_g,
                w_s, b_s, conv_mix_w, conv_mix_b, out_norm_a_g, out_norm_b_g, w_out, norm_ffn_g,
                w_gate, w_up, conv_ffn_w, conv_ffn_b, w_down, final_norm_g,
                y_prompt, y_sample, new_mix_prompt, new_ffn_prompt, new_mix_sample, new_ffn_sample,
                new_chunk_v):
    _, SEQ, DM = x_prompt.shape
    NB, NS, _ = x_sample.shape
    FF = w_gate.shape[2]
    AW = sgu_norm_g.shape[1]
    assert w_s.shape[2] == P and AW % P == 0 and conv_mix_b.shape[1] == AW and DM == 2 * AW
    SAMP = NB * NS
    T = SEQ + SAMP
    HALF = T // 2
    KT = DM // P
    HEADS = AW // P
    TB = SEQ // P
    FT = FF // P
    NBLK = FT // 2
    PK = KT // 2
    IN_TILES = w_in.shape[2] // P
    IN_PIECES = 2 * IN_TILES
    GEMM_PIECES = IN_PIECES + 2 * KT
    ZP = 2 + SEQ + NB * (2 + NS)
    CV = ZP - 2
    ROWS = 2 + 2 * NB
    EPS = 1e-6

    ctx = ExitStack()
    with ctx:
        def psum(name, shape):
            return ctx.enter_context(nc.psum_tensor(name, shape, F32))

        def sem(name):
            return ctx.enter_context(nc.semaphore(name))

        base = -(-nc.sbuf_base // 32) * 32
        ARENA = 212800
        ctx.enter_context(nc.sbuf_tensor("arena", [P, ARENA // 4], F32))
        place = [base]

        def sb(name, shape, dt=F32, at=None):
            n = 4
            for s in shape[1:]:
                n *= s
            n = -(-n // 32) * 32
            off = place[0] if at is None else at
            if at is None:
                place[0] += n
                assert place[0] <= base + ARENA, (name, place[0] - base)
            return nc.alloc_sbuf_tensor_at(name, shape, dt, offset=off)

        h_at = place[0]
        h_hi = sb("h_hi", [P, KT, T], F32R)
        h_lo = sb("h_lo", [P, KT, T], F32R)
        X = sb("X", [P, KT, T])
        n_at = place[0]
        x_nat = sb("x_nat", [P, 2, DM])
        ws_nat = sb("ws_nat", [P, HEADS, P], at=n_at)
        ffn_nat = sb("ffn_nat", [FT, 4 + 2 * NB, P], at=n_at + 4096)
        v_nat = sb("v_nat", [P, 2, TB + 1, P], at=n_at)
        ffn_rows = sb("ffn_rows", [P, ROWS, FT], at=n_at)
        ffn_stage = sb("ffn_stage", [FT, ROWS, P], at=n_at + 4096)
        mix_stage = sb("mix_stage", [P, 2, P], at=n_at + 14336)
        raw = sb("raw", [P, 2, PK, P])
        w_hi = sb("w_hi", [P, 4, PK, P], F32R)
        w_lo = sb("w_lo", [P, 4, PK, P], F32R)
        q_at = place[0]
        wsT = sb("wsT", [P, HEADS, P])
        ws_blk = sb("ws_blk", [SAMP, HEADS, NB, NS])
        bias_b = sb("bias_b", [P, HEADS, P])
        act_hi = sb("act_hi", [P, 2, T], F32R, at=q_at)
        act_lo = sb("act_lo", [P, 2, T], F32R, at=q_at + 8 * T)
        out_nat = sb("out_nat", [P, TB + 1, DM], at=h_at)

        scaled = sb("scaled", [P, T])
        u_gelu = sb("u_gelu", [P, T])
        prod = sb("prod", [P, T])
        sq = sb("sq", [P, T])
        psq = sb("psq", [P, T])
        acc = sb("acc", [P, T])
        rms = sb("rms", [P, T])
        rb = sb("rb", [P, T])
        zpad = sb("zpad", [P, ZP])
        cv = sb("cv", [P, CV])
        vn_at = place[0]
        vn = sb("vn", [P, T])
        gate_act = sb("gate_act", [P, CV], at=vn_at)
        place[0] += 64
        ident = sb("ident", [P, P])
        ones = sb("ones", [P, P])
        vec_nat = sb("vec_nat", [P, P])
        mix_rows = sb("mix_rows", [P, ROWS, HEADS])
        vecs = sb("vecs", [P, 104])
        mixst_nat = sb("mixst_nat", [P, P])
        mixst = sb("mixst", [P, 2 * NB, HEADS])
        ffnv = sb("ffnv", [P, 4 + 2 * NB, FT])
        small = sb("small", [P, 32])
        sel = sb("sel", [P, NB, NS])
        rv = psq
        ssq_nat = small[:, 0:TB + 1]
        rms_nat = small[:, 8:8 + TB + 1]
        eps_t = small[:, 16:17]
        blk_mask = small[0:SAMP, 24:24 + NB]
        fin_g = [scaled, u_gelu]
        fin_sq = [sq, prod]

        G_MIX, G_FFN, G_FIN, G_SGU, G_OUT, MIX_W, MIX_B = 0, 16, 32, 48, 56, 72, 96

        ps = psum("ps", [P, 8, 512])

        def pair(p, half):
            return ps[:, 2 * p + half, 0:HALF]

        T_BANK, SSQ_BANK, MIX_BANK = 4, 5, 6
        t_samp = ps[0:SAMP, 7, 0:128]
        ssq_samp = ps[:, 7, 128:192]
        mix_samp = ps[:, 7, 192:256]

        raw_landed = [sem(f"raw_landed{i}") for i in range(2)]
        hi_ready = sem("hi_ready")
        lo_ready = sem("lo_ready")
        piece_done = sem("piece_done")
        down_done = sem("down_done")
        down_added = sem("down_added")
        xnat_landed = [sem(f"xnat_landed{i}") for i in range(2)]
        consts_ready = sem("consts_ready")
        vecs_landed = sem("vecs_landed")
        late_landed = sem("late_landed")
        vec_t = sem("vec_t")
        vec_ready = sem("vec_ready")
        x_t = sem("x_t")
        xT_copied = sem("xT_copied")
        xg_ready = sem("xg_ready")
        xhi_ready = sem("xhi_ready")
        xlo_ready = sem("xlo_ready")
        ssqn_ready = sem("ssqn_ready")
        diag_ready = sem("diag_ready")
        scratch_out = sem("scratch_out")
        resid_in = sem("resid_in")
        ssq_done = sem("ssq_done")
        rms_ready = sem("rms_ready")
        rrms_ready = sem("rrms_ready")
        tile_read = sem("tile_read")
        gelu_done = sem("gelu_done")
        acc_done = sem("acc_done")
        param_t = sem("param_t")
        param_ready = sem("param_ready")
        ws_masked = sem("ws_masked")
        sel_ready = sem("sel_ready")
        corner_done = sem("corner_done")
        blk_ready = sem("blk_ready")
        vn_ready = sem("vn_ready")
        v_t = sem("v_t")
        v_ready = sem("v_ready")
        v_out = [sem(f"v_out{i}") for i in range(2)]
        mix_done = sem("mix_done")
        mix_read = sem("mix_read")
        y_raw = sem("y_raw")
        y_sq = sem("y_sq")
        y_ready = sem("y_ready")
        yhi_ready = sem("yhi_ready")
        ylo_ready = sem("ylo_ready")
        hhi_ready = sem("hhi_ready")
        hlo_ready = sem("hlo_ready")
        z_ready = sem("z_ready")
        pads_ready = sem("pads_ready")
        rows_saved = sem("rows_saved")
        tap2_done = sem("tap2_done")
        tap1_done = sem("tap1_done")
        conv_done = sem("conv_done")
        silu_done = sem("silu_done")
        up_read = sem("up_read")
        act_prod = sem("act_prod")
        acthi_ready = sem("acthi_ready")
        act_ready = sem("act_ready")
        rows_t = sem("rows_t")
        rows_staged = sem("rows_staged")
        rows_out = sem("rows_out")
        fsq_ready = sem("fsq_ready")
        fg_ready = sem("fg_ready")
        facc_done = sem("facc_done")
        f_t = sem("f_t")
        f_ready = sem("f_ready")
        fssq_done = sem("fssq_done")
        frms_ready = sem("frms_ready")
        frrms_ready = sem("frrms_ready")
        out_d = sem("out_d")
        out_a = sem("out_a")
        stored = sem("stored")
        stored_sp = sem("stored_sp")

        scratch = nc.dram_tensor("xT_scratch", [P, KT * T], F32).ap()

        xp, xs = x_prompt[0], x_sample.rearrange("b s d -> (b s) d")
        zs = zpad[:, 2 + SEQ:ZP].rearrange("p (b t) -> p b t", b=NB)

        def samp8(ap):
            return ap.rearrange("p (b t) -> p b t", b=NB)

        def conv_samp(buf):
            return buf[:, SEQ:SEQ + NB * (NS + 2)].rearrange("p (b t) -> p b t", b=NB)[:, :, 2:NS + 2]

        assert CV == SEQ + NB * (NS + 2)

        def blk_q(b):
            return b * 12 + (GEMM_PIECES - 4)

        def blk_p(b):
            return b * 8 + GEMM_PIECES

        block = ctx.enter_context(nc.Block())

        @block.sync
        def _(sp):
            def load(q, c, src, first=False):
                if not first:
                    sp.wait_ge(lo_ready, q - 1)
                dst = raw[:, c % 2]
                if len(src.shape) == 3 and src.shape[2] != P:
                    dst = dst.rearrange("p (k j) c -> p k (j c)", k=2)
                sp.dma_start(dst, src).then_inc(raw_landed[c % 2], 16)

            def col(w, n, half):
                return w[0][half * PK * P:(half + 1) * PK * P, ds(n * P, P)].rearrange("(k p) c -> p k c", p=P)

            def down(b, d):
                return w_down[0][ds(b * (2 * P), 2 * P), d * 4 * P:(d + 1) * 4 * P].rearrange("(k p) c -> p k c", p=P)

            def tile2(w, n, q, first=False):
                for half in range(2):
                    load(q + half, half, col(w, n, half), first=first)

            tile2(w_in, HEADS, 0, first=True)
            tile2(w_in, HEADS + 1, 2)
            with sp.Fori(1, HEADS // 2) as i:
                for s in range(2):
                    tile2(w_in, i * 2 + (HEADS + s), i * 4 + 2 * s)
            with sp.Fori(0, HEADS // 2) as i:
                for s in range(2):
                    tile2(w_in, i * 2 + s, i * 4 + (2 * HEADS + 2 * s))
            with sp.Fori(0, HEADS) as i:
                for s, part in enumerate((4, 3, 2)):
                    tile2(w_in, i + part * HEADS, i * 6 + (4 * HEADS + 2 * s))
            with sp.Fori(0, KT) as i:
                tile2(w_out, i, i * 2 + IN_PIECES)
            for c, (w, f) in enumerate(((w_gate, 0), (w_up, 0), (w_gate, 1), (w_up, 1))):
                tile2(w, f, GEMM_PIECES + 2 * c)
            with sp.Fori(1, NBLK) as b:
                tile2(w_gate, b * 2, blk_q(b))
                for d in range(4):
                    load(blk_q(b) + 2 + d, d, down(b - 1, d))
                tile2(w_up, b * 2, blk_q(b) + 6)
                tile2(w_gate, b * 2 + 1, blk_q(b) + 8)
                tile2(w_up, b * 2 + 1, blk_q(b) + 10)
            for d in range(4):
                load(blk_q(NBLK) + d, d, down(NBLK - 1, d))

            for n, tb in enumerate((1, 3)):
                sp.wait_ge(out_a, n + 1)
                sp.dma_start(y_prompt[0][tb * P:(tb + 1) * P, :], out_nat[:, tb, :]).then_inc(stored_sp, 16)
            sp.wait_ge(rows_out, 4 * 16)
            sp.wait_ge(v_out[0], 16 * HEADS // 2)
            sp.wait_ge(v_out[1], 16 * HEADS // 2)
            sp.wait_ge(stored_sp, 2 * 16)
            sp.wait_ge(stored, 3 * 16)

        @block.gpsimd
        def _(pool):
            g = nc.gpsimd
            g.dma_start(x_nat[:, 0, :], xp[0:P, :]).then_inc(xnat_landed[0], 16)
            g.dma_start(x_nat[:, 1, :], xp[P:2 * P, :]).then_inc(xnat_landed[1], 16)
            rows = ((G_MIX, norm_mix_g[0], 16), (G_FFN, norm_ffn_g[0], 16), (G_FIN, final_norm_g, 16),
                    (G_SGU, sgu_norm_g[0], 8), (G_OUT, out_norm_a_g[0], 8), (G_OUT + 8, out_norm_b_g[0], 8),
                    (MIX_B, conv_mix_b[0], 8))
            for at, v, n in rows:
                g.dma_start(vec_nat[at:at + n, :], v.rearrange("(t c) -> t c", c=P)).then_inc(vecs_landed, 16)
            g.dma_start(vec_nat[MIX_W:MIX_W + 24, :],
                        conv_mix_w[0].rearrange("k (t c) -> (k t) c", c=P)).then_inc(vecs_landed, 16)
            g.dma_start(mixst_nat[:, :],
                        state_conv_mix[0].rearrange("b k (t c) -> (b k t) c", c=P)).then_inc(vecs_landed, 16)
            g.memset(ident[:, :], 0.0).then_inc(consts_ready, 1)
            g.memset(ones[:, :], 1.0).then_inc(consts_ready, 1)
            g.memset(small[:, :], EPS).then_inc(consts_ready, 1)
            g.memset(zpad[:, :], 0.0).then_inc(consts_ready, 1)
            g.memset(acc[:, :], 0.0).then_inc(consts_ready, 1)
            pool.wait_ge(consts_ready, 5)
            g.affine_select(out=ident[:, :], in_=ident[:, :], compare_op=ALU.not_equal, fill=1.0, base=0,
                            pattern=[[-1, P]], channel_multiplier=1).then_inc(consts_ready, 1)
            g.memset(blk_mask, 1.0).then_inc(consts_ready, 1)
            pool.wait_ge(consts_ready, 7)
            g.affine_select(out=blk_mask, in_=blk_mask, compare_op=ALU.is_ge, fill=0.0, base=0,
                            pattern=[[-NS, NB]], channel_multiplier=1).then_inc(consts_ready, 1)
            pool.wait_ge(consts_ready, 8)
            g.affine_select(out=blk_mask, in_=blk_mask, compare_op=ALU.is_ge, fill=0.0, base=NS - 1,
                            pattern=[[NS, NB]], channel_multiplier=-1).then_inc(consts_ready, 1)

            def x_lo(u, kq, tok, n):
                src = (scaled, u_gelu)[kq % 2][:, 0:4 * n].rearrange("p (k t) -> p k t", k=4)
                hi = h_hi[:, 4 * kq:4 * kq + 4, ds(tok, n)].bitcast(F32)
                pool.wait_ge(xhi_ready, u + 1)
                g.tensor_tensor(h_lo[:, 4 * kq:4 * kq + 4, ds(tok, n)], src, hi,
                                ALU.subtract).then_inc(xlo_ready, 1)

            for tb in range(TB + 1):
                for kq in range(4):
                    x_lo(4 * tb + kq, kq, tb * P, P if tb < TB else SAMP)
                nxt = tb + 2
                if nxt <= TB:
                    pool.wait_ge(x_t, 4 * tb + 4)
                    pool.wait_ge(ssqn_ready, tb + 1)
                    if nxt < TB:
                        g.dma_start(x_nat[:, nxt % 2, :], xp[nxt * P:(nxt + 1) * P, :]).then_inc(xnat_landed[nxt % 2], 16)
                    else:
                        g.dma_start(x_nat[0:SAMP, nxt % 2, :], xs).then_inc(xnat_landed[nxt % 2], 16)
            pool.wait_ge(xT_copied, 4 * (TB + 1))
            g.dma_start(scratch, X[:, :, :].rearrange("p k t -> p (k t)")).then_inc(scratch_out, 16)
            pool.wait_ge(x_t, 4 * (TB + 1))
            pool.wait_ge(ssqn_ready, TB + 1)
            g.dma_start(ws_nat[:, :, :], w_s[0].rearrange("h i j -> i h j")).then_inc(late_landed, 16)
            g.dma_start(ffn_nat[:, 0:3, :], conv_ffn_w[0].rearrange("k (t c) -> t k c", c=P)).then_inc(late_landed, 16)
            g.dma_start(ffn_nat[:, 3, :], conv_ffn_b[0].rearrange("(t c) -> t c", c=P)).then_inc(late_landed, 16)
            g.dma_start(ffn_nat[:, 4:, :],
                        state_conv_ffn[0].rearrange("b k (t c) -> t (b k) c", c=P)).then_inc(late_landed, 16)
            g.dma_start(bias_b[:, :, :].rearrange("p h i -> p (h i)"),
                        b_s[0].rearrange("h i -> (h i)").rearrange("(a n) -> a n", a=1).broadcast_to([P, HEADS * P])
                        ).then_inc(late_landed, 16)

            def square_sum(k, done, count):
                pool.wait_ge(*done)
                g.tensor_tensor(psq[:, :], X[:, ds(k, 1), :].rearrange("p a t -> p (a t)"),
                                X[:, ds(k, 1), :].rearrange("p a t -> p (a t)"), ALU.mult).then_inc(acc_done, 1)
                pool.wait_ge(acc_done, count + 1)
                g.tensor_tensor(acc[:, :], acc[:, :], psq[:, :], ALU.add).then_inc(acc_done, 1)
                pool.wait_ge(acc_done, count + 2)

            for i in range(2):
                square_sum(i, (gelu_done, i + 1), 2 * i)
            pool.wait_ge(param_ready, 2)
            g.affine_select(out=wsT[:, :, :], in_=wsT[:, :, :], compare_op=ALU.is_ge, fill=0.0, base=0,
                            pattern=[[0, HEADS], [1, P]], channel_multiplier=-1).then_inc(ws_masked, 1)
            with pool.Fori(2, HEADS) as i:
                square_sum(i, (gelu_done, i + 1), i * 2)
            pool.wait_ge(ssq_done, 2)
            g.memset(acc[:, :], 0.0).then_inc(acc_done, 1)
            vc = new_chunk_v[0].rearrange("b s c -> (b s) c")
            with pool.Fori(0, HEADS // 2) as i:
                for s in range(2):
                    pool.wait_ge(v_ready, i * 2 + (s + 1))
                    g.dma_start(vc[:, ds(i * (2 * P) + s * P, P)], v_nat[0:SAMP, s, TB, :]).then_inc(v_out[s], 16)

            def conv_pads(k, src):
                pool.wait_ge(pads_free(k), k)
                g.tensor_copy(zs[:, :, 0:2], src).then_inc(pads_ready, 1)

            def pads_free(k):
                return conv_done

            def save_rows(k, dst, i):
                pool.wait_ge(z_ready, k + 1)
                g.tensor_copy(dst[:, 0:2, ds(i, 1)].rearrange("p r a -> p (r a)"), zpad[:, SEQ:SEQ + 2])
                g.tensor_copy(dst[:, 2:, ds(i, 1)].rearrange("p (b k) a -> p b (k a)", b=NB),
                              zs[:, :, NS:NS + 2]).then_inc(rows_saved, 1)

            def mix_state(i):
                return mixst[:, :, ds(i, 1)].rearrange("p (b k) a -> p b (k a)", b=NB)

            def ffn_state(f):
                return ffnv[:, 4:, ds(f, 1)].rearrange("p (b k) a -> p b (k a)", b=NB)

            pool.wait_ge(vec_ready, 2)
            g.tensor_copy(zs[:, :, 0:2], mix_state(0)).then_inc(pads_ready, 1)
            save_rows(0, mix_rows, 0)
            with pool.Fori(1, HEADS) as i:
                conv_pads(i, mix_state(i))
                save_rows(i, mix_rows, i)
            for s in range(4):
                pool.wait_ge(ylo_ready, 4 * s + 4)
                g.dma_start(X[:, 4 * s:4 * s + 4, :].rearrange("p k t -> p (k t)"),
                            scratch[:, 4 * s * T:(4 * s + 4) * T]).then_inc(resid_in, 16)
            with pool.Fori(0, KT) as m:
                square_sum(m, (tile_read, m + (IN_TILES + 1)), m * 2 + (2 * HEADS + 1))
            with pool.Fori(0, FT) as f:
                conv_pads(f + HEADS, ffn_state(f))
                save_rows(f + HEADS, ffn_rows, f)
            pool.wait_ge(rms_ready, 3 + KT)
            g.memset(acc[:, :], 0.0).then_inc(facc_done, 1)
            pool.wait_ge(rows_staged, 1)
            g.dma_start(new_ffn_prompt[0, 0].rearrange("r (t c) -> t r c", c=P), ffn_stage[:, 0:2, :]).then_inc(rows_out, 16)
            g.dma_start(new_ffn_sample[0].rearrange("b k (t c) -> t (b k) c", c=P), ffn_stage[:, 2:, :]).then_inc(rows_out, 16)
            g.dma_start(new_mix_prompt[0, 0].rearrange("r (t c) -> (r t) c", c=P), mix_stage[0:16, 0, :]).then_inc(rows_out, 16)
            g.dma_start(new_mix_sample[0].rearrange("b k (t c) -> (b k t) c", c=P), mix_stage[:, 1, :]).then_inc(rows_out, 16)
            pool.wait_ge(facc_done, 1)
            with pool.Fori(0, KT // 2) as j:
                for s in range(2):
                    pool.wait_ge(fsq_ready, j * 2 + (s + 1))
                    g.tensor_tensor(acc[:, :], acc[:, :], fin_sq[s][:, :], ALU.add).then_inc(facc_done, 1)
                    pool.wait_ge(facc_done, j * 2 + (s + 2))
            for n, tb in enumerate((0, 2, 4)):
                pool.wait_ge(out_d, n + 1)
                if tb < TB:
                    g.dma_start(y_prompt[0][tb * P:(tb + 1) * P, :], out_nat[:, tb, :]).then_inc(stored, 16)
                else:
                    g.dma_start(y_sample.rearrange("b s d -> (b s) d"), out_nat[0:SAMP, tb, :]).then_inc(stored, 16)

        @block.scalar
        def _(act):
            a = nc.scalar

            def split_hi(q, c, free=None):
                if free is not None:
                    act.wait_ge(*free)
                act.wait_ge(raw_landed[c % 2], landed(q, c))
                a.activation(w_hi[:, c % 4], raw[:, c % 2], ACT.Copy).then_inc(hi_ready, 1)

            def landed(q, c):
                return (q - c % 2) * 8 + 16

            def root(n, scale, prev):
                act.wait_ge(ssq_done, n)
                if prev is not None:
                    act.wait_ge(*prev)
                a.activation(rms[:, 0:SEQ], ps[:, SSQ_BANK, :], ACT.Sqrt, bias=eps_t, scale=scale)
                a.activation(rms[:, SEQ:T], ssq_samp, ACT.Sqrt, bias=eps_t, scale=scale).then_inc(rms_ready, 1)

            act.wait_ge(vec_t, 1)
            a.activation(vecs[:, :], ps[:, 0, 0:104], ACT.Copy).then_inc(vec_ready, 1)
            a.activation(mixst[:, :, :].rearrange("p r t -> p (r t)"), ps[:, 0, 128:256], ACT.Copy).then_inc(vec_ready, 1)
            for tb in range(TB + 1):
                n = P if tb < TB else SAMP
                for kq in range(4):
                    act.wait_ge(x_t, 4 * tb + kq + 1)
                    a.activation(X[:, 4 * kq:4 * kq + 4, tb * P:tb * P + n],
                                 ps[:, 4 + kq, 0:4 * n].rearrange("p (k t) -> p k t", k=4),
                                 ACT.Copy).then_inc(xT_copied, 1)
                act.wait_ge(vec_ready, 2)
                if tb >= 1:
                    act.wait_ge(ssqn_ready, tb)
                a.activation(ps[0:n, 0:4, :].rearrange("p a b -> p (a b)"), x_nat[0:n, tb % 2, :], ACT.Square,
                             accum_out=ssq_nat[0:n, tb:tb + 1]).then_inc(ssqn_ready, 1)
                if tb == 1:
                    for c in range(2):
                        split_hi(c, c)
            for c in range(2, 4):
                split_hi(c, c)
            root(1, 1.0 / DM, None)

            def gelu_v(i, t):
                act.wait_ge(tile_read, t + 1)
                a.activation(X[:, ds(i, 1), :].rearrange("p a t -> p (a t)"), scaled[:, :],
                             ACT.Gelu_apprx_tanh).then_inc(gelu_done, 1)

            def split2_hi(q, c, done):
                for s in range(2):
                    split_hi(q + s, c + s, (piece_done, done + s))

            act.wait_ge(scratch_out, 16)
            for i in range(2):
                gelu_v(i, i)
                split2_hi(2 * i + 4, 2 * i, 2 * i + 1)
                if i == 1:
                    act.wait_ge(param_t, 1)
                    for n in range(2):
                        a.activation(wsT[:, 4 * n:4 * n + 4, :].rearrange("p h i -> p (h i)"), ps[:, 4 + n, :],
                                     ACT.Copy).then_inc(param_ready, 1)
                    a.activation(ffnv[:, 0:11, :].rearrange("p r t -> p (r t)"), ps[:, 6, 0:11 * FT],
                                 ACT.Copy).then_inc(param_ready, 1)
                    a.activation(ffnv[:, 11:, :].rearrange("p r t -> p (r t)"), ps[:, 7, 0:9 * FT],
                                 ACT.Copy).then_inc(param_ready, 1)
            with act.Fori(1, HEADS // 2) as i:
                for s in range(2):
                    gelu_v(i * 2 + s, i * 2 + s)
                    split2_hi(i * 4 + (2 * s + 4), 2 * s, i * 4 + (2 * s + 1))

            def gelu_u(i):
                act.wait_ge(tile_read, i + (HEADS + 1))
                a.activation(u_gelu[:, :], scaled[:, :], ACT.Gelu_apprx_tanh).then_inc(gelu_done, 1)

            def v_store(i, s):
                act.wait_ge(v_t, i + 1)
                a.activation(v_nat[:, s, 0:TB, :].rearrange("p b d -> p (b d)"), ps[:, T_BANK, :], ACT.Copy)
                a.activation(v_nat[0:SAMP, s, TB, :], t_samp, ACT.Copy).then_inc(v_ready, 1)

            root(2, 1.0 / AW, (rrms_ready, 1))
            gelu_u(0)
            v_store(0, 0)
            split2_hi(2 * HEADS + 4, 0, 2 * HEADS + 1)
            act.wait_ge(y_raw, 1)
            gelu_u(1)
            v_store(1, 1)
            root(3, 1.0 / P, (rrms_ready, 2))
            split2_hi(2 * HEADS + 6, 2, 2 * HEADS + 3)
            with act.Fori(1, HEADS // 2) as i:
                for s in range(2):
                    n = i * 2 + (s + 1)
                    act.wait_ge(y_raw, n - 1)
                    gelu_u(n - 1)
                    act.wait_ge(mix_done, n - 2)
                    act.wait_ge(v_out[s], i * 16)
                    v_store(n - 1, s)
                    root(n + 1, 1.0 / P, (y_ready, n - 2))
                    split2_hi(i * 4 + (2 * HEADS + 4 + 2 * s), 2 * s, i * 4 + (2 * HEADS + 1 + 2 * s))

            def tap2(k, w, b, prev):
                act.wait_ge(z_ready, k + 1)
                act.wait_ge(pads_ready, k + 1)
                if prev is not None:
                    act.wait_ge(*prev)
                a.activation(cv[:, :], zpad[:, 2:ZP], ACT.Identity, bias=b, scale=w).then_inc(tap2_done, 1)

            def group_b(i, first, last_c):
                q = i * 6 + 4 * HEADS
                root(i + (HEADS + 2), 1.0 / P, (y_ready, i + (HEADS - 1)))
                split2_hi(q + 4, last_c, q + 1)
                tap2(i, vecs[:, ds(i + (MIX_W + 16), 1)], vecs[:, ds(i + MIX_B, 1)],
                     None if first == "first" else (y_raw, i + HEADS))
                split2_hi(q + 6, last_c + 2, q + 3)
                split2_hi(q + 8, last_c, q + 5)

            group_b(0, "first", 0)
            group_b(1, None, 2)
            with act.Fori(1, HEADS // 2) as i:
                group_b(i * 2, None, 0)
                group_b(i * 2 + 1, None, 2)

            def y_hi(k):
                act.wait_ge(y_ready, k + 1)
                a.activation(h_hi[:, ds(k, 1), :].rearrange("p a t -> p (a t)"),
                             X[:, ds(k, 1), :].rearrange("p a t -> p (a t)"), ACT.Copy).then_inc(yhi_ready, 1)

            act.wait_ge(piece_done, IN_PIECES)
            with act.Fori(0, 4) as k:
                y_hi(k)
            root(2 + KT, 1.0 / P, (y_ready, KT - 1))
            with act.Fori(4, KT) as k:
                y_hi(k)
            with act.Fori(0, KT // 2) as i:
                for s in range(2):
                    split2_hi(i * 4 + (IN_PIECES + 4 + 2 * s), 2 * s, i * 4 + (IN_PIECES + 1 + 2 * s))
            act.wait_ge(piece_done, GEMM_PIECES)

            def h_hi_k(k):
                act.wait_ge(tile_read, k + (IN_TILES + 1))
                a.activation(h_hi[:, ds(k, 1), :].rearrange("p a t -> p (a t)"),
                             X[:, ds(k, 1), :].rearrange("p a t -> p (a t)"), ACT.Copy,
                             scale=vecs[:, ds(k + G_FFN, 1)]).then_inc(hhi_ready, 1)

            with act.Fori(0, KT) as k:
                h_hi_k(k)
            root(3 + KT, 1.0 / DM, (y_ready, KT))

            def gate(f, q, c, done, first=False):
                tap2(f + HEADS, ffnv[:, 2, ds(f, 1)], ffnv[:, 3, ds(f, 1)], None)
                split2_hi(q, c, done)
                act.wait_ge(conv_done, f + (HEADS + 1))
                if not first:
                    act.wait_ge(act_prod, f)
                a.activation(gate_act[:, :], cv[:, :], ACT.Silu).then_inc(silu_done, 1)

            def up(f, s):
                act.wait_ge(act_prod, f + 1)
                a.activation(act_hi[:, s, :], prod[:, :], ACT.Copy).then_inc(acthi_ready, 1)

            gate(0, GEMM_PIECES + 4, 0, GEMM_PIECES + 1, first=True)
            up(0, 0)
            split2_hi(GEMM_PIECES + 6, 2, GEMM_PIECES + 3)
            gate(1, blk_q(1), 0, GEMM_PIECES + 5)
            up(1, 1)
            split2_hi(blk_q(1) + 2, 2, GEMM_PIECES + 7)
            with act.Fori(1, NBLK) as b:
                q, p, d = blk_q(b), blk_p(b), (b - 1) * 16
                gate(b * 2, q + 4, 0, p + 1)
                for c in range(4):
                    split_hi(q + 6 + c, 2 + c, (down_done, d + 4 * (c + 1)))
                up(b * 2, 0)
                split2_hi(q + 10, 2, p + 3)
                gate(b * 2 + 1, blk_q(b + 1), 0, p + 5)
                up(b * 2 + 1, 1)
                split2_hi(blk_q(b + 1) + 2, 2, p + 7)

            act.wait_ge(rows_t, 1)
            flat = ffn_stage[:, :, :].rearrange("t r c -> t (r c)")
            for n in range(5):
                m = min(512, ROWS * P - 512 * n)
                a.activation(flat[:, 512 * n:512 * n + m], ps[0:FT, n, 0:m], ACT.Copy)
            a.activation(mix_stage[0:16, 0, :], ps[0:16, 4, 256:384], ACT.Copy)
            a.activation(mix_stage[:, 1, :], ps[:, 4, 384:512], ACT.Copy).then_inc(rows_staged, 1)
            D0 = (NBLK - 1) * 16

            def last_tile(j, s, first):
                act.wait_ge(down_added, j + (D0 + 1))
                xj = X[:, ds(j, 1), :].rearrange("p a t -> p (a t)")
                if not first:
                    act.wait_ge(facc_done, j)
                a.activation(fin_sq[s][:, :], xj, ACT.Square).then_inc(fsq_ready, 1)
                if not first:
                    act.wait_ge(f_t, j - 1)
                a.activation(fin_g[s][:, :], xj, ACT.Copy, scale=vecs[:, ds(j + G_FIN, 1)]).then_inc(fg_ready, 1)

            for s in range(2):
                last_tile(s, s, True)
            with act.Fori(1, KT // 2) as i:
                for s in range(2):
                    last_tile(i * 2 + s, s, False)
            act.wait_ge(fssq_done, 1)
            a.activation(rms_nat[:, 0:TB], ps[:, 0, 0:TB], ACT.Sqrt, bias=eps_t, scale=1.0 / DM)
            a.activation(rms_nat[0:SAMP, TB:TB + 1], ps[0:SAMP, 0, TB:TB + 1], ACT.Sqrt, bias=eps_t[0:SAMP],
                         scale=1.0 / DM).then_inc(frms_ready, 1)
            act.wait_ge(frrms_ready, 1)
            act.wait_ge(f_ready, KT)
            for tb in (1, 3):
                a.activation(out_nat[:, tb, :], out_nat[:, tb, :], ACT.Copy,
                             scale=rms_nat[:, tb:tb + 1]).then_inc(out_a, 1)

        @block.vector
        def _(dve):
            v = nc.vector

            def row(buf, k):
                return buf[:, ds(k, 1), :].rearrange("p a t -> p (a t)")

            def split_lo(q, c):
                dve.wait_ge(hi_ready, q + 1)
                v.tensor_tensor(w_lo[:, c % 4], raw[:, c % 2], w_hi[:, c % 4].bitcast(F32),
                                ALU.subtract).then_inc(lo_ready, 1)

            def split2_lo(q, c):
                for s in range(2):
                    split_lo(q + s, c + s)

            def times_rb(dst, p, done):
                v.tensor_tensor(dst[:, 0:HALF], pair(p, 0), rb[:, 0:HALF], ALU.mult)
                v.tensor_tensor(dst[:, HALF:T], pair(p, 1), rb[:, HALF:T], ALU.mult).then_inc(done, 1)

            def reciprocal_rms(n, dst):
                dve.wait_ge(rms_ready, n)
                v.reciprocal(dst[:, :], rms[:, :]).then_inc(rrms_ready, 1)

            dve.wait_ge(vec_ready, 1)
            for tb in range(TB + 1):
                n = P if tb < TB else SAMP
                for kq in range(4):
                    u = 4 * tb + kq
                    dve.wait_ge(xT_copied, u + 1)
                    if u >= 2:
                        dve.wait_ge(xlo_ready, u - 1)
                    xg = (scaled, u_gelu)[u % 2][:, 0:4 * n].rearrange("p (k t) -> p k t", k=4)
                    gain = vecs[:, G_MIX + 4 * kq:G_MIX + 4 * kq + 4].rearrange("p (k a) -> p k a", a=1).broadcast_to([P, 4, n])
                    v.tensor_tensor(xg, X[:, 4 * kq:4 * kq + 4, tb * P:tb * P + n], gain,
                                    ALU.mult).then_inc(xg_ready, 1)
                    dve.wait_ge(xg_ready, u + 1)
                    v.tensor_copy(h_hi[:, 4 * kq:4 * kq + 4, tb * P:tb * P + n], xg).then_inc(xhi_ready, 1)
                if tb == 1:
                    split2_lo(0, 0)
            dve.wait_ge(ssqn_ready, TB + 1)
            dve.wait_ge(consts_ready, 9)
            for tb in range(TB + 1):
                n = P if tb < TB else SAMP
                d = v.tensor_scalar(sq[0:n, tb * P:tb * P + n], ident[0:n, 0:n], ssq_nat[0:n, tb:tb + 1], None, ALU.mult)
            d.then_inc(diag_ready, 1)
            split2_lo(2, 2)
            v.tensor_copy(sel[:, :, :], ident[:, 0:NS].rearrange("p (a j) -> p a j", a=1).broadcast_to([P, NB, NS])
                          ).then_inc(sel_ready, 1)
            reciprocal_rms(1, rb)
            dve.wait_ge(rrms_ready, 1)
            dve.wait_ge(xlo_ready, 4 * (TB + 1))

            def v_tile(t, s, first=False):
                dve.wait_ge(piece_done, t * 2 + 2)
                if not first:
                    dve.wait_ge(gelu_done, t)
                times_rb(scaled, s, tile_read)

            for t in range(2):
                v_tile(t, t, first=t == 0)
                split2_lo(2 * t + 4, 2 * t)
            with dve.Fori(1, HEADS // 2) as i:
                for s in range(2):
                    v_tile(i * 2 + s, s)
                    split2_lo(i * 4 + (2 * s + 4), 2 * s)

            dve.wait_ge(corner_done, 1)
            v.tensor_tensor(ws_blk[:, :, :, :],
                            ps[0:SAMP, 4, 0:SAMP].rearrange("p (h a i) -> p h a i", h=HEADS, a=1).broadcast_to([SAMP, HEADS, NB, NS]),
                            blk_mask.rearrange("p (a b c) -> p a b c", a=1, c=1).broadcast_to([SAMP, HEADS, NB, NS]),
                            ALU.mult).then_inc(blk_ready, 1)

            def norm_v(i):
                v.scalar_tensor_tensor(out=vn[:, :], in0=row(X, i), scalar=vecs[:, ds(i + G_SGU, 1)],
                                       in1=rv[:, :], op0=ALU.mult, op1=ALU.mult).then_inc(vn_ready, 1)

            def square_y(n):
                dve.wait_ge(y_raw, n + 1)
                dve.wait_ge(ssq_done, n + 2)
                v.tensor_tensor(sq[:, :], row(X, n), row(X, n), ALU.mult).then_inc(y_sq, 1)

            def norm_y(n):
                reciprocal_rms_inplace(n)
                v.scalar_tensor_tensor(out=row(X, n), in0=row(X, n), scalar=vecs[:, ds(n + G_OUT, 1)],
                                       in1=rms[:, :], op0=ALU.mult, op1=ALU.mult).then_inc(y_ready, 1)

            def reciprocal_rms_inplace(n):
                reciprocal_rms(n + 3, rms)
                dve.wait_ge(rrms_ready, n + 3)

            def gate_a(i):
                dve.wait_ge(mix_done, i + 1)
                bi = bias_b[:, ds(i, 1), :]
                v.tensor_tensor(prod[:, 0:SEQ].rearrange("p (c t) -> p c t", c=TB),
                                ps[:, MIX_BANK, :].rearrange("p (c t) -> p c t", c=TB),
                                bi.broadcast_to([P, TB, P]), ALU.add)
                v.tensor_tensor(samp8(prod[:, SEQ:T]), samp8(mix_samp),
                                bias_b[:, ds(i, 1), 0:NS].broadcast_to([P, NB, NS]), ALU.add).then_inc(mix_read, 1)
                dve.wait_ge(mix_read, i + 1)
                dve.wait_ge(gelu_done, i + (HEADS + 1))
                v.tensor_tensor(row(X, i), prod[:, :], u_gelu[:, :], ALU.mult).then_inc(y_raw, 1)
                square_y(i)

            dve.wait_ge(acc_done, 2 * HEADS + 1)
            dve.wait_ge(rms_ready, 2)
            v.reciprocal(rv[:, :], rms[:, :]).then_inc(rrms_ready, 1)
            dve.wait_ge(rrms_ready, 2)
            dve.wait_ge(late_landed, 5 * 16)
            norm_v(0)

            def u_tile(i, s):
                dve.wait_ge(piece_done, i * 2 + (2 * HEADS + 2))
                dve.wait_ge(gelu_done, i + HEADS)
                times_rb(scaled, s, tile_read)

            u_tile(0, 0)
            split2_lo(2 * HEADS + 4, 0)
            dve.wait_ge(v_t, 1)
            norm_v(1)
            gate_a(0)
            u_tile(1, 1)
            split2_lo(2 * HEADS + 6, 2)
            dve.wait_ge(v_t, 2)
            norm_v(2)
            norm_y(0)
            gate_a(1)
            with dve.Fori(1, HEADS // 2 - 1) as i:
                for s in range(2):
                    n = i * 2 + (s + 1)
                    u_tile(n - 1, s)
                    split2_lo(i * 4 + (2 * HEADS + 4 + 2 * s), 2 * s)
                    dve.wait_ge(v_t, n)
                    norm_v(n)
                    norm_y(n - 2)
                    gate_a(n - 1)
            u_tile(HEADS - 2, 0)
            split2_lo(4 * HEADS, 0)
            dve.wait_ge(v_t, HEADS - 1)
            norm_v(HEADS - 1)
            norm_y(HEADS - 3)
            gate_a(HEADS - 2)
            u_tile(HEADS - 1, 1)
            split2_lo(4 * HEADS + 2, 2)
            norm_y(HEADS - 2)
            gate_a(HEADS - 1)

            def conv_taps(k, w1, w0):
                dve.wait_ge(tap2_done, k + 1)
                v.scalar_tensor_tensor(out=cv[:, :], in0=zpad[:, 1:ZP - 1], scalar=w1, in1=cv[:, :],
                                       op0=ALU.mult, op1=ALU.add).then_inc(tap1_done, 1)
                dve.wait_ge(tap1_done, k + 1)
                v.scalar_tensor_tensor(out=cv[:, :], in0=zpad[:, 0:ZP - 2], scalar=w0, in1=cv[:, :],
                                       op0=ALU.mult, op1=ALU.add).then_inc(conv_done, 1)

            def group_b(i, first, c):
                t = i * 3 + 2 * HEADS
                q = t * 2
                dve.wait_ge(piece_done, q + 2)
                if first:
                    dve.wait_ge(gelu_done, 2 * HEADS)
                times_rb(scaled, (c // 2) % 2, tile_read)
                split2_lo(q + 4, c)
                norm_y(i + (HEADS - 1))
                dve.wait_ge(piece_done, q + 4)
                times_rb(prod, (c // 2 + 1) % 2, tile_read)
                dve.wait_ge(tile_read, t + 2)
                if first:
                    dve.wait_ge(pads_ready, 1)
                else:
                    dve.wait_ge(rows_saved, i)
                v.tensor_tensor(zpad[:, 2:2 + SEQ], prod[:, 0:SEQ], scaled[:, 0:SEQ], ALU.mult)
                v.tensor_tensor(zs[:, :, 2:], samp8(prod[:, SEQ:T]), samp8(scaled[:, SEQ:T]),
                                ALU.mult).then_inc(z_ready, 1)
                split2_lo(q + 6, c + 2)
                conv_taps(i, vecs[:, ds(i + (MIX_W + 8), 1)], vecs[:, ds(i + MIX_W, 1)])
                dve.wait_ge(piece_done, q + 6)
                dve.wait_ge(z_ready, i + 1)
                times_rb(prod, (c // 2) % 2, tile_read)
                dve.wait_ge(tile_read, t + 3)
                dve.wait_ge(conv_done, i + 1)
                yi = X[:, ds(i + HEADS, 1), :].rearrange("p a t -> p (a t)")
                v.tensor_tensor(yi[:, 0:SEQ], prod[:, 0:SEQ], cv[:, 0:SEQ], ALU.mult)
                v.tensor_tensor(samp8(yi[:, SEQ:T]), samp8(prod[:, SEQ:T]), conv_samp(cv), ALU.mult).then_inc(y_raw, 1)
                square_y(i + HEADS)
                split2_lo(q + 8, c)

            group_b(0, True, 0)
            group_b(1, False, 2)
            with dve.Fori(1, HEADS // 2) as i:
                group_b(i * 2, False, 0)
                group_b(i * 2 + 1, False, 2)

            def y_lo(k):
                dve.wait_ge(yhi_ready, k + 1)
                v.tensor_tensor(row(h_lo, k), row(X, k), row(h_hi, k).bitcast(F32), ALU.subtract).then_inc(ylo_ready, 1)

            with dve.Fori(0, 4) as k:
                y_lo(k)
            norm_y(KT - 1)
            with dve.Fori(4, KT) as k:
                y_lo(k)

            def w_out_tile(m, s):
                dve.wait_ge(piece_done, m * 2 + (IN_PIECES + 2))
                xm = row(X, m)
                v.tensor_tensor(xm[:, 0:HALF], xm[:, 0:HALF], pair(s, 0), ALU.add)
                v.tensor_tensor(xm[:, HALF:T], xm[:, HALF:T], pair(s, 1), ALU.add).then_inc(tile_read, 1)

            split2_lo(IN_PIECES + 4, 0)
            dve.wait_ge(resid_in, 4 * 16)
            w_out_tile(0, 0)
            split2_lo(IN_PIECES + 6, 2)
            w_out_tile(1, 1)
            with dve.Fori(1, KT // 2) as i:
                for s in range(2):
                    split2_lo(i * 4 + (IN_PIECES + 4 + 2 * s), 2 * s)
                    w_out_tile(i * 2 + s, s)

            def h_lo_k(k):
                dve.wait_ge(hhi_ready, k + 1)
                v.scalar_tensor_tensor(out=row(h_lo, k), in0=row(X, k), scalar=vecs[:, ds(k + G_FFN, 1)],
                                       in1=row(h_hi, k).bitcast(F32), op0=ALU.mult,
                                       op1=ALU.subtract).then_inc(hlo_ready, 1)

            with dve.Fori(0, KT) as k:
                h_lo_k(k)
            reciprocal_rms(3 + KT, rb)
            dve.wait_ge(rrms_ready, 3 + KT)

            def gate_in(f, p, done):
                dve.wait_ge(piece_done, done)
                dve.wait_ge(rows_saved, f + HEADS)
                n = SEQ - HALF
                v.tensor_tensor(zpad[:, 2:2 + HALF], pair(p, 0), rb[:, 0:HALF], ALU.mult)
                v.tensor_tensor(zpad[:, 2 + HALF:2 + SEQ], ps[:, 2 * p + 1, 0:n], rb[:, HALF:SEQ], ALU.mult)
                v.tensor_tensor(zs[:, :, 2:], samp8(ps[:, 2 * p + 1, n:HALF]), samp8(rb[:, SEQ:T]),
                                ALU.mult).then_inc(z_ready, 1)

            def gate_conv(f):
                conv_taps(f + HEADS, ffnv[:, 1, ds(f, 1)], ffnv[:, 0, ds(f, 1)])

            def up_in(f, p, done, s, first=False):
                dve.wait_ge(piece_done, done)
                if not first:
                    dve.wait_ge(act_ready, f)
                times_rb(scaled, p, up_read)
                dve.wait_ge(up_read, f + 1)
                dve.wait_ge(silu_done, f + 1)
                v.tensor_tensor(prod[:, 0:SEQ], scaled[:, 0:SEQ], gate_act[:, 0:SEQ], ALU.mult)
                v.tensor_tensor(samp8(prod[:, SEQ:T]), samp8(scaled[:, SEQ:T]), conv_samp(gate_act),
                                ALU.mult).then_inc(act_prod, 1)
                dve.wait_ge(acthi_ready, f + 1)
                v.tensor_tensor(act_lo[:, s, :], prod[:, :], act_hi[:, s, :].bitcast(F32),
                                ALU.subtract).then_inc(act_ready, 1)

            def down_add(j, p, done):
                dve.wait_ge(down_done, done)
                v.tensor_tensor(X[:, j, 0:HALF], X[:, j, 0:HALF], pair(p, 0), ALU.add)
                v.tensor_tensor(X[:, j, HALF:T], X[:, j, HALF:T], pair(p, 1), ALU.add).then_inc(down_added, 1)

            g0 = GEMM_PIECES
            gate_in(0, 0, g0 + 2)
            split2_lo(g0 + 4, 0)
            gate_conv(0)
            up_in(0, 1, g0 + 4, 0, first=True)
            split2_lo(g0 + 6, 2)
            gate_in(1, 2, g0 + 6)
            split2_lo(blk_q(1), 0)
            gate_conv(1)
            up_in(1, 3, g0 + 8, 1)
            split2_lo(blk_q(1) + 2, 2)
            with dve.Fori(1, NBLK) as b:
                q, p, d = blk_q(b), blk_p(b), (b - 1) * 16
                gate_in(b * 2, 0, p + 2)
                split2_lo(q + 4, 0)
                gate_conv(b * 2)
                for j in range(16):
                    down_add(j, (j + 1) % 4, d + (j + 1))
                    if j % 4 == 3:
                        split_lo(q + 6 + j // 4, 2 + j // 4)
                up_in(b * 2, 1, p + 4, 0)
                split2_lo(q + 10, 2)
                gate_in(b * 2 + 1, 2, p + 6)
                split2_lo(blk_q(b + 1), 0)
                gate_conv(b * 2 + 1)
                up_in(b * 2 + 1, 3, p + 8, 1)
                split2_lo(blk_q(b + 1) + 2, 2)

            D0 = (NBLK - 1) * 16
            dve.wait_ge(piece_done, blk_p(NBLK))

            def out_store(j, s):
                dve.wait_ge(f_t, j + 1)
                v.tensor_copy(out_nat[:, 0:TB, j * P:(j + 1) * P],
                              ps[:, 4 + 2 * s, :].rearrange("p (b c) -> p b c", b=TB))
                v.tensor_copy(out_nat[0:SAMP, TB, j * P:(j + 1) * P], ps[0:SAMP, 5 + 2 * s, 0:P]).then_inc(f_ready, 1)

            for j in range(16):
                down_add(j, j % 2, D0 + j + 1)
                if j >= 2:
                    out_store(j - 2, j % 2)
            out_store(14, 0)
            out_store(15, 1)
            dve.wait_ge(frms_ready, 1)
            v.reciprocal(rms_nat[:, 0:TB], rms_nat[:, 0:TB])
            v.reciprocal(rms_nat[0:SAMP, TB:TB + 1], rms_nat[0:SAMP, TB:TB + 1]).then_inc(frrms_ready, 1)
            dve.wait_ge(frrms_ready, 1)
            dve.wait_ge(f_ready, KT)
            for tb in (0, 2, 4):
                n = P if tb < TB else SAMP
                v.tensor_scalar(out_nat[0:n, tb, :], out_nat[0:n, tb, :], rms_nat[0:n, tb:tb + 1], None,
                                ALU.mult).then_inc(out_d, 1)

        @block.tensor
        def _(pe):
            t_ = nc.tensor

            def three(out, whi, wlo, xhi, xlo, start, stop):
                t_.matmul(out, whi, xhi, start=start, stop=False)
                t_.matmul(out, whi, xlo, start=False, stop=False)
                return t_.matmul(out, wlo, xhi, start=False, stop=stop)

            def gemm(q, c, p, q1=None, mid=None, q3=None):
                for half in range(2):
                    cols = slice(half * HALF, (half + 1) * HALF)
                    for s in range(2):
                        if half == 0:
                            pe.wait_ge(lo_ready, q + s + 1)
                        for k in range(PK):
                            kk = s * PK + k
                            last = three(pair(p, half), w_hi[:, (c + s) % 4, k, :], w_lo[:, (c + s) % 4, k, :],
                                         h_hi[:, kk, cols], h_lo[:, kk, cols], kk == 0, kk == KT - 1)
                        if half == 1:
                            last.then_inc(piece_done, 1)
                        hook = (q1, mid, q3, None)[2 * half + s]
                        if hook is not None:
                            hook()

            def gemm_by_k(q, c, p, ready, mid=None):
                for kk in range(KT):
                    s, k = kk // PK, kk % PK
                    if k == 0:
                        pe.wait_ge(lo_ready, q + s + 1)
                    pe.wait_ge(ready, kk + 1)
                    for half in range(2):
                        cols = slice(half * HALF, (half + 1) * HALF)
                        last = three(pair(p, half), w_hi[:, (c + s) % 4, k, :], w_lo[:, (c + s) % 4, k, :],
                                     h_hi[:, kk, cols], h_lo[:, kk, cols], kk == 0, kk == KT - 1)
                    if k == PK - 1:
                        last.then_inc(piece_done, 1)
                    if kk == PK - 1 and mid is not None:
                        mid()

            def ssq(src, n):
                t_.matmul(ps[:, SSQ_BANK, :], ones[:, :], src[:, 0:SEQ], start=True, stop=True)
                t_.matmul(ssq_samp, ones[:, :], src[:, SEQ:T], start=True, stop=True).then_inc(ssq_done, 1)

            pe.wait_ge(consts_ready, 6)
            pe.wait_ge(vecs_landed, 9 * 16)
            t_.transpose(ps[:, 0, 0:104], vec_nat[0:104, :], ident[0:104, 0:104])
            t_.transpose(ps[:, 0, 128:256], mixst_nat[:, :], ident[:, :]).then_inc(vec_t, 1)
            for tb in range(TB + 1):
                n = P if tb < TB else SAMP
                pe.wait_ge(xnat_landed[tb % 2], 16 * (tb // 2 + 1))
                for kq in range(4):
                    u = 4 * tb + kq
                    if tb >= 1:
                        pe.wait_ge(xT_copied, u - 3)
                    for k in range(4):
                        last = t_.transpose(ps[:, 4 + kq, k * n:(k + 1) * n],
                                            x_nat[0:n, tb % 2, (4 * kq + k) * P:(4 * kq + k + 1) * P], ident[0:n, 0:n])
                    last.then_inc(x_t, 1)

            def spread_x_ssq():
                pe.wait_ge(diag_ready, 1)
                pe.wait_ge(xT_copied, 4 * (TB + 1))
                for tb in range(TB):
                    t_.matmul(ps[:, SSQ_BANK, tb * P:(tb + 1) * P], ones[:, :], sq[:, tb * P:(tb + 1) * P],
                              start=True, stop=True)
                t_.matmul(ssq_samp, ones[0:SAMP, :], sq[0:SAMP, SEQ:T], start=True, stop=True).then_inc(ssq_done, 1)

            def params_t():
                pe.wait_ge(late_landed, 5 * 16)
                pe.wait_ge(rms_ready, 1)
                for h in range(HEADS):
                    t_.transpose(ps[:, 4 + h // 4, (h % 4) * P:(h % 4 + 1) * P], ws_nat[:, h, :], ident[:, :])
                for r in range(4 + 2 * NB):
                    b, c = (6, r) if r < 11 else (7, r - 11)
                    last = t_.transpose(ps[:, b, c * FT:(c + 1) * FT], ffn_nat[:, r, :], ident[0:FT, 0:FT])
                last.then_inc(param_t, 1)

            def corner():
                pe.wait_ge(ws_masked, 1)
                pe.wait_ge(sel_ready, 1)
                pe.wait_ge(param_ready, 4)
                t_.matmul(ps[0:SAMP, 4, 0:SAMP], sel[:, :, :].rearrange("p b j -> p (b j)"), wsT[:, :, 0:NS],
                          start=True, stop=True).then_inc(corner_done, 1)

            pe.wait_ge(xlo_ready, 4 * (TB + 1))
            pe.wait_ge(ssqn_ready, TB + 1)
            gemm(0, 0, 0, mid=spread_x_ssq)
            gemm(2, 2, 1, mid=params_t)
            for t in (2, 3):
                pe.wait_ge(tile_read, t - 1)
                gemm(2 * t, 2 * t, t % 2, mid=corner if t == 3 else None)
            with pe.Fori(2, HEADS // 2) as i:
                for s in range(2):
                    pe.wait_ge(tile_read, i * 2 + (s - 1))
                    gemm(i * 4 + 2 * s, 2 * s, s)

            def v_transposes(i, first=False):
                pe.wait_ge(vn_ready, i + 1)
                if not first:
                    pe.wait_ge(v_ready, i)
                    pe.wait_ge(mix_read, i)
                for b in range(TB):
                    t_.transpose(ps[:, T_BANK, b * P:(b + 1) * P], vn[:, b * P:(b + 1) * P], ident[:, :])
                t_.transpose(t_samp, vn[:, SEQ:T], ident[:, :]).then_inc(v_t, 1)

            def mix(i, s, roots):
                pe.wait_ge(v_ready, i + 1)
                pe.wait_ge(rms_ready, roots)
                for b in range(TB):
                    t_.matmul(ps[:, MIX_BANK, b * P:(b + 1) * P], v_nat[:, s, b, :],
                              wsT[:, ds(i, 1), :].rearrange("p a i -> p (a i)"), start=True, stop=True)
                t_.matmul(mix_samp, v_nat[0:SAMP, s, TB, :],
                          ws_blk[:, ds(i, 1), :, :].rearrange("p a b i -> p (a b i)"),
                          start=True, stop=True).then_inc(mix_done, 1)

            def y_ssq(n):
                pe.wait_ge(y_sq, n + 1)
                pe.wait_ge(rms_ready, n + 2)
                ssq(sq, n + 3)

            def v_ssq():
                pe.wait_ge(acc_done, 2 * HEADS)
                ssq(acc, 2)

            q0 = 2 * HEADS
            pe.wait_ge(tile_read, HEADS - 1)
            gemm(q0, 0, 0, mid=v_ssq)
            pe.wait_ge(tile_read, HEADS)
            pe.wait_ge(blk_ready, 1)
            v_transposes(0, first=True)
            gemm(q0 + 2, 2, 1, q3=lambda: mix(0, 0, 2))

            def step_u(i, s, q):
                pe.wait_ge(tile_read, i + (HEADS - 1))
                v_transposes(i - 1)

                def sums():
                    pe.wait_ge(v_ready, i)
                    y_ssq(i - 2)

                gemm(q, 2 * s, s, q1=sums, q3=lambda: mix(i - 1, 1 - s, i + 1))

            with pe.Fori(1, HEADS // 2) as i:
                step_u(i * 2, 0, i * 4 + q0)
                step_u(i * 2 + 1, 1, i * 4 + (q0 + 2))

            def group_b(i, t, q, c, mids):
                for s in range(3):
                    pe.wait_ge(tile_read, t + (s - 1))
                    gemm(q + 2 * s, c + 2 * s, (c // 2 + s) % 2, mid=mids[s])

            step_u(HEADS, 0, 4 * HEADS)
            pe.wait_ge(tile_read, 2 * HEADS)

            def last_of_a():
                pe.wait_ge(mix_read, HEADS)
                y_ssq(HEADS - 1)

            gemm(4 * HEADS + 2, 2, 1, mid=last_of_a)
            pe.wait_ge(tile_read, 2 * HEADS + 1)
            gemm(4 * HEADS + 4, 0, 0)
            group_b(1, 2 * HEADS + 3, 4 * HEADS + 6, 2, (lambda: y_ssq(HEADS), None, None))
            with pe.Fori(1, HEADS // 2) as i:
                for s in range(2):
                    group_b(None, i * 6 + (2 * HEADS + 3 * s), i * 12 + (4 * HEADS + 6 * s), 2 * s,
                            (lambda: y_ssq(i * 2 + (HEADS - 1 + s)), None, None))

            y_ssq(KT - 1)
            pe.wait_ge(tile_read, IN_TILES - 1)
            gemm_by_k(IN_PIECES, 0, 0, ylo_ready)
            pe.wait_ge(tile_read, IN_TILES)
            gemm(IN_PIECES + 2, 2, 1)
            with pe.Fori(1, KT // 2) as i:
                for s in range(2):
                    pe.wait_ge(tile_read, i * 2 + (IN_TILES - 1 + s))
                    gemm(i * 4 + (IN_PIECES + 2 * s), 2 * s, s)

            def x_ssq():
                pe.wait_ge(acc_done, 2 * HEADS + 1 + 2 * KT)
                pe.wait_ge(rms_ready, KT + 2)
                ssq(acc, KT + 3)

            def down_tile(slot, jj, p):
                for half in range(2):
                    cols = slice(half * HALF, (half + 1) * HALF)
                    for k in range(2):
                        last = three(pair(p, half), w_hi[:, slot, 4 * k + jj, :], w_lo[:, slot, 4 * k + jj, :],
                                     act_hi[:, k, cols], act_lo[:, k, cols], k == 0, k == 1)
                last.then_inc(down_done, 1)

            g0 = GEMM_PIECES
            pe.wait_ge(tile_read, IN_TILES + KT - 1)
            gemm_by_k(g0, 0, 0, hlo_ready, mid=x_ssq)
            pe.wait_ge(tile_read, IN_TILES + KT)
            gemm(g0 + 2, 2, 1)
            pe.wait_ge(rms_ready, KT + 3)
            gemm(g0 + 4, 0, 2)
            gemm(g0 + 6, 2, 3)

            def ffn_block(b, first):
                q, d = blk_q(b), (b - 1) * 16
                pe.wait_ge(*((z_ready, HEADS + 1) if first else (down_added, d)))
                gemm(q, 0, 0)
                pe.wait_ge(act_ready, b * 2)
                for j in range(16):
                    if j % 4 == 0:
                        pe.wait_ge(lo_ready, q + 3 + j // 4)
                    if j == 0:
                        pe.wait_ge(up_read, b * 2 - 1)
                    elif j == 1:
                        pe.wait_ge(z_ready, b * 2 + HEADS)
                    elif j == 2:
                        pe.wait_ge(up_read, b * 2)
                    elif j == 3:
                        pe.wait_ge(z_ready, b * 2 + (HEADS + 1))
                    else:
                        pe.wait_ge(down_added, d + (j - 3))
                    down_tile((2 + j // 4) % 4, j % 4, (j + 1) % 4)
                pe.wait_ge(down_added, d + 13)
                gemm(q + 6, 2, 1)
                pe.wait_ge(down_added, d + 14)
                gemm(q + 8, 0, 2)
                pe.wait_ge(down_added, d + 15)
                gemm(q + 10, 2, 3)

            ffn_block(1, True)
            with pe.Fori(2, NBLK) as b:
                ffn_block(b, False)

            D0 = (NBLK - 1) * 16
            pe.wait_ge(rows_saved, HEADS + FT)
            pe.wait_ge(down_added, D0)
            pe.wait_ge(up_read, FT - 1)
            pe.wait_ge(z_ready, HEADS + FT)
            for r in range(ROWS):
                t_.transpose(ps[0:FT, r // 4, (r % 4) * P:(r % 4 + 1) * P], ffn_rows[:, r, :], ident[:, :])
            t_.transpose(ps[0:16, 4, 256:384], mix_rows[:, 0:2, :].rearrange("p r t -> p (r t)"), ident[:, :])
            t_.transpose(ps[:, 4, 384:512], mix_rows[:, 2:, :].rearrange("p r t -> p (r t)"), ident[:, :]).then_inc(rows_t, 1)
            pe.wait_ge(act_ready, FT)
            pe.wait_ge(rows_staged, 1)
            pe.wait_ge(up_read, FT)

            def out_t(j):
                s = j % 2
                pe.wait_ge(fg_ready, j + 1)
                if j >= 2:
                    pe.wait_ge(f_ready, j - 1)
                for b in range(TB):
                    t_.transpose(ps[:, 4 + 2 * s, b * P:(b + 1) * P], fin_g[s][:, b * P:(b + 1) * P], ident[:, :])
                t_.transpose(ps[0:SAMP, 5 + 2 * s, 0:P], fin_g[s][:, SEQ:T], ident[:, :]).then_inc(f_t, 1)

            for j in range(16):
                if j % 4 == 0:
                    pe.wait_ge(lo_ready, blk_q(NBLK) + j // 4 + 1)
                if j >= 2:
                    pe.wait_ge(down_added, D0 + j - 1)
                down_tile(j // 4, j % 4, j % 2)
                if j >= 2:
                    out_t(j - 2)
            out_t(14)
            out_t(15)
            pe.wait_ge(facc_done, KT + 1)
            pe.wait_ge(down_added, D0 + 16)
            for tb in range(TB + 1):
                n = P if tb < TB else SAMP
                last = t_.matmul(ps[0:n, 0, tb:tb + 1], acc[:, tb * P:tb * P + n], ones[:, 0:1], start=True, stop=True)
            last.then_inc(fssq_done, 1)


_INS = ["x_prompt", "x_sample", "state_conv_mix", "state_conv_ffn", "norm_mix_g", "w_in", "sgu_norm_g", "w_s",
        "b_s", "conv_mix_w", "conv_mix_b", "out_norm_a_g", "out_norm_b_g", "w_out", "norm_ffn_g", "w_gate",
        "w_up", "conv_ffn_w", "conv_ffn_b", "w_down", "final_norm_g"]
_OUTS = [(1, 512, 2048), (8, 8, 2048), (1, 1, 2, 1024), (1, 1, 2, 5632), (1, 8, 2, 1024), (1, 8, 2, 5632),
         (1, 8, 8, 1024)]


def kernel(**inputs):
    import numpy as _np
    import concourse.bacc as _bacc
    from concourse import mybir as _mybir
    from concourse.bass_utils import run_bass_kernel_spmd as _run

    nc = _bacc.Bacc("TRN2", target_bir_lowering=False, num_devices=1)
    arrays, args = {}, []
    for name in _INS:
        a = _np.ascontiguousarray(inputs[name])
        arrays[f"in_{name}_dram"] = a
        args.append(nc.dram_tensor(f"in_{name}_dram", a.shape, _mybir.dt.from_np(a.dtype), kind="ExternalInput").ap())
    for i, shape in enumerate(_OUTS):
        args.append(nc.dram_tensor(f"out_{i}_dram", shape, F32, kind="ExternalOutput").ap())
    build_layer(nc, *args)
    r = _run(nc, [arrays], core_ids=[0])
    return tuple(r.results[0][f"out_{i}_dram"] for i in range(len(_OUTS)))
```

```python
from contextlib import ExitStack

import concourse.bass as bass
from concourse import mybir

F32 = mybir.dt.float32
F32R = mybir.dt.float32r
ALU = mybir.AluOpType
ACT = mybir.ActivationFunctionType
ds = bass.ds

P = 128


def build_layer(nc, x_prompt, x_sample, state_conv_mix, state_conv_ffn, norm_mix_g, w_in, sgu_norm_g,
                w_s, b_s, conv_mix_w, conv_mix_b, out_norm_a_g, out_norm_b_g, w_out, norm_ffn_g,
                w_gate, w_up, conv_ffn_w, conv_ffn_b, w_down, final_norm_g,
                y_prompt, y_sample, new_mix_prompt, new_ffn_prompt, new_mix_sample, new_ffn_sample,
                new_chunk_v):
    _, SEQ, DM = x_prompt.shape
    NB, NS, _ = x_sample.shape
    FF = w_gate.shape[2]
    AW = sgu_norm_g.shape[1]
    assert w_s.shape[2] == P and AW % P == 0 and conv_mix_b.shape[1] == AW and DM == 2 * AW
    SAMP = NB * NS
    T = SEQ + SAMP
    HALF = T // 2
    KT = DM // P
    HEADS = AW // P
    TB = SEQ // P
    FT = FF // P
    NBLK = FT // 2
    PK = KT // 2
    IN_TILES = w_in.shape[2] // P
    IN_PIECES = 2 * IN_TILES
    GEMM_PIECES = IN_PIECES + 2 * KT
    ZP = 2 + SEQ + NB * (2 + NS)
    CV = ZP - 2
    ROWS = 2 + 2 * NB
    EPS = 1e-6

    ctx = ExitStack()
    with ctx:
        def psum(name, shape):
            return ctx.enter_context(nc.psum_tensor(name, shape, F32))

        def sem(name):
            return ctx.enter_context(nc.semaphore(name))

        base = -(-nc.sbuf_base // 32) * 32
        ARENA = 212800
        ctx.enter_context(nc.sbuf_tensor("arena", [P, ARENA // 4], F32))
        place = [base]

        def sb(name, shape, dt=F32, at=None):
            n = 4
            for s in shape[1:]:
                n *= s
            n = -(-n // 32) * 32
            off = place[0] if at is None else at
            if at is None:
                place[0] += n
                assert place[0] <= base + ARENA, (name, place[0] - base)
            return nc.alloc_sbuf_tensor_at(name, shape, dt, offset=off)

        h_at = place[0]
        h_hi = sb("h_hi", [P, KT, T], F32R)
        h_lo = sb("h_lo", [P, KT, T], F32R)
        X = sb("X", [P, KT, T])
        n_at = place[0]
        x_nat = [sb("x_nat0", [P, DM]), sb("x_nat1", [P, DM])]
        ws_nat = sb("ws_nat", [P, HEADS, P], at=n_at)
        ffn_nat = sb("ffn_nat", [FT, 4 + 2 * NB, P], at=n_at + 4096)
        v_nat = sb("v_nat", [P, 2, TB + 1, P], at=n_at)
        ffn_rows = sb("ffn_rows", [P, ROWS, FT], at=n_at)
        ffn_stage = sb("ffn_stage", [FT, ROWS, P], at=n_at + 4096)
        mix_stage = sb("mix_stage", [P, 2, P], at=n_at + 14336)
        raw = sb("raw", [P, 2, PK, P])
        w_at = place[0]
        w_hi = sb("w_hi", [P, 4, PK, P], F32R)
        w_lo = sb("w_lo", [P, 4, PK, P], F32R)
        q_at = place[0]
        x_nat.append(sb("x_nat2", [P, DM], at=q_at))
        wsT = sb("wsT", [P, HEADS, P])
        ws_blk = sb("ws_blk", [SAMP, HEADS, NB, NS])
        bias_b = sb("bias_b", [P, HEADS, P])
        act_hi = sb("act_hi", [P, 2, T], F32R, at=q_at)
        act_lo = sb("act_lo", [P, 2, T], F32R, at=q_at + 8 * T)
        out_nat = sb("out_nat", [P, TB + 1, DM], at=h_at)

        scaled = sb("scaled", [P, T])
        u_gelu = sb("u_gelu", [P, T])
        prod_at = place[0]
        x_nat.append(sb("x_nat3", [P, DM], at=prod_at))
        x_nat.append(sb("x_nat4", [P, DM], at=w_at + 2 * PK * P * 4))
        prod = sb("prod", [P, T])
        sq_at = place[0]
        sq = sb("sq", [P, T])
        sq_lo = sb("sq_lo", [P, T], F32R, at=sq_at)
        psq = sb("psq", [P, T])
        acc_at = place[0]
        acc = sb("acc", [P, T])
        sq_hi = sb("sq_hi", [P, T], F32R, at=acc_at)
        rms = sb("rms", [P, T])
        rb = sb("rb", [P, T])
        zpad = sb("zpad", [P, ZP])
        cv = sb("cv", [P, CV])
        vn_at = place[0]
        vn = sb("vn", [P, T])
        gate_act = sb("gate_act", [P, CV], at=vn_at)
        place[0] += 64
        ident = sb("ident", [P, P])
        ones_r = sb("ones_r", [P, P], F32R)
        ones = ones_r[:, :].bitcast(F32)
        vec_nat = sb("vec_nat", [P, P])
        mix_rows = sb("mix_rows", [P, ROWS, HEADS])
        vecs = sb("vecs", [P, 104])
        mixst_nat = sb("mixst_nat", [P, P])
        mixst = sb("mixst", [P, 2 * NB, HEADS])
        ffnv = sb("ffnv", [P, 4 + 2 * NB, FT])
        small = sb("small", [P, 32])
        sel = sb("sel", [P, NB, NS])
        rv = psq
        ssq_nat = small[:, 0:TB + 1]
        rms_nat = small[:, 8:8 + TB + 1]
        eps_t = small[:, 16:17]
        blk_mask = small[0:SAMP, 24:24 + NB]
        xg_bufs = [scaled, u_gelu, rms, rb]
        fin_g = [scaled, u_gelu]
        fin_sq = [sq, prod]

        G_MIX, G_FFN, G_FIN, G_SGU, G_OUT, MIX_W, MIX_B = 0, 16, 32, 48, 56, 72, 96

        ps = psum("ps", [P, 8, 512])

        def pair(p, half):
            return ps[:, 2 * p + half, 0:HALF]

        T_BANK, SSQ_BANK, MIX_BANK = 4, 5, 6
        t_samp = ps[0:SAMP, 7, 0:128]
        ssq_samp = ps[:, 7, 128:192]
        mix_samp = ps[:, 7, 192:256]

        raw_landed = [sem(f"raw_landed{i}") for i in range(2)]
        hi_ready = sem("hi_ready")
        lo_ready = sem("lo_ready")
        piece_done = sem("piece_done")
        down_done = sem("down_done")
        down_added = sem("down_added")
        xnat_landed = [sem(f"xnat_landed{i}") for i in range(TB + 1)]
        consts_ready = sem("consts_ready")
        gain_landed = sem("gain_landed")
        vecs_landed = sem("vecs_landed")
        late_landed = sem("late_landed")
        vec_t = sem("vec_t")
        vec_ready = sem("vec_ready")
        x_t = sem("x_t")
        xT_copied = sem("xT_copied")
        xg_ready = sem("xg_ready")
        xhi_ready = sem("xhi_ready")
        xlo_pool = sem("xlo_pool")
        xlo_dve = sem("xlo_dve")
        ones_ready = sem("ones_ready")
        ssqn_ready = sem("ssqn_ready")
        diag_ready = sem("diag_ready")
        scratch_out = sem("scratch_out")
        resid_in = sem("resid_in")
        ssq_done = sem("ssq_done")
        rms_ready = sem("rms_ready")
        rrms_ready = sem("rrms_ready")
        tile_read = sem("tile_read")
        gelu_done = sem("gelu_done")
        acc_done = sem("acc_done")
        param_t = sem("param_t")
        param_ready = sem("param_ready")
        ws_masked = sem("ws_masked")
        sel_ready = sem("sel_ready")
        corner_done = sem("corner_done")
        blk_ready = sem("blk_ready")
        vn_ready = sem("vn_ready")
        v_t = sem("v_t")
        v_ready = sem("v_ready")
        v_out = [sem(f"v_out{i}") for i in range(2)]
        mix_done = sem("mix_done")
        mix_read = sem("mix_read")
        y_raw = sem("y_raw")
        y_sq = sem("y_sq")
        y_ready = sem("y_ready")
        yhi_ready = sem("yhi_ready")
        ylo_ready = sem("ylo_ready")
        hhi_ready = sem("hhi_ready")
        hlo_ready = sem("hlo_ready")
        z_ready = sem("z_ready")
        pads_ready = sem("pads_ready")
        rows_saved = sem("rows_saved")
        tap2_done = sem("tap2_done")
        tap1_done = sem("tap1_done")
        conv_done = sem("conv_done")
        silu_done = sem("silu_done")
        up_read = sem("up_read")
        act_prod = sem("act_prod")
        acthi_ready = sem("acthi_ready")
        act_ready = sem("act_ready")
        rows_t = sem("rows_t")
        rows_staged = sem("rows_staged")
        rows_out = sem("rows_out")
        fsq_ready = sem("fsq_ready")
        fg_ready = sem("fg_ready")
        facc_done = sem("facc_done")
        f_t = sem("f_t")
        f_ready = sem("f_ready")
        fssq_done = sem("fssq_done")
        frms_ready = sem("frms_ready")
        frrms_ready = sem("frrms_ready")
        out_d = sem("out_d")
        out_a = sem("out_a")
        stored = sem("stored")
        stored_sp = sem("stored_sp")

        scratch = nc.dram_tensor("xT_scratch", [P, KT * T], F32).ap()

        xp, xs = x_prompt[0], x_sample.rearrange("b s d -> (b s) d")
        zs = zpad[:, 2 + SEQ:ZP].rearrange("p (b t) -> p b t", b=NB)

        def samp8(ap):
            return ap.rearrange("p (b t) -> p b t", b=NB)

        def conv_samp(buf):
            return buf[:, SEQ:SEQ + NB * (NS + 2)].rearrange("p (b t) -> p b t", b=NB)[:, :, 2:NS + 2]

        assert CV == SEQ + NB * (NS + 2)

        def xg_of(kq, n):
            return xg_bufs[kq][:, 0:4 * n].rearrange("p (k t) -> p k t", k=4)

        def blk_q(b):
            return b * 12 + (GEMM_PIECES - 4)

        def blk_p(b):
            return b * 8 + GEMM_PIECES

        block = ctx.enter_context(nc.Block())

        @block.sync
        def _(sp):
            def load(q, c, src, first=False):
                if not first:
                    sp.wait_ge(lo_ready, q - 1)
                dst = raw[:, c % 2]
                if len(src.shape) == 3 and src.shape[2] != P:
                    dst = dst.rearrange("p (k j) c -> p k (j c)", k=2)
                sp.dma_start(dst, src).then_inc(raw_landed[c % 2], 16)

            def col(w, n, half):
                return w[0][half * PK * P:(half + 1) * PK * P, ds(n * P, P)].rearrange("(k p) c -> p k c", p=P)

            def down(b, d):
                return w_down[0][ds(b * (2 * P), 2 * P), d * 4 * P:(d + 1) * 4 * P].rearrange("(k p) c -> p k c", p=P)

            def tile2(w, n, q, first=False):
                for half in range(2):
                    load(q + half, half, col(w, n, half), first=first)

            sp.dma_start(vec_nat[0:KT, :], norm_mix_g[0].rearrange("(t c) -> t c", c=P)).then_inc(gain_landed, 16)
            for tb in range(TB + 1):
                if tb < TB:
                    sp.dma_start(x_nat[tb][:, :], xp[tb * P:(tb + 1) * P, :]).then_inc(xnat_landed[tb], 16)
                else:
                    sp.dma_start(x_nat[tb][0:SAMP, :], xs).then_inc(xnat_landed[tb], 16)
                if tb == 1:
                    tile2(w_in, HEADS, 0, first=True)
            tile2(w_in, HEADS + 1, 2)
            with sp.Fori(1, HEADS // 2) as i:
                for s in range(2):
                    tile2(w_in, i * 2 + (HEADS + s), i * 4 + 2 * s)
            with sp.Fori(0, HEADS // 2) as i:
                for s in range(2):
                    tile2(w_in, i * 2 + s, i * 4 + (2 * HEADS + 2 * s))
            with sp.Fori(0, HEADS) as i:
                for s, part in enumerate((4, 3, 2)):
                    tile2(w_in, i + part * HEADS, i * 6 + (4 * HEADS + 2 * s))
            with sp.Fori(0, KT) as i:
                tile2(w_out, i, i * 2 + IN_PIECES)
            for c, (w, f) in enumerate(((w_gate, 0), (w_up, 0), (w_gate, 1), (w_up, 1))):
                tile2(w, f, GEMM_PIECES + 2 * c)
            with sp.Fori(1, NBLK) as b:
                tile2(w_gate, b * 2, blk_q(b))
                for d in range(4):
                    load(blk_q(b) + 2 + d, d, down(b - 1, d))
                tile2(w_up, b * 2, blk_q(b) + 6)
                tile2(w_gate, b * 2 + 1, blk_q(b) + 8)
                tile2(w_up, b * 2 + 1, blk_q(b) + 10)
            for d in range(4):
                load(blk_q(NBLK) + d, d, down(NBLK - 1, d))

            for n, tb in enumerate((1, 3)):
                sp.wait_ge(out_a, n + 1)
                sp.dma_start(y_prompt[0][tb * P:(tb + 1) * P, :], out_nat[:, tb, :]).then_inc(stored_sp, 16)
            sp.wait_ge(rows_out, 4 * 16)
            sp.wait_ge(v_out[0], 16 * HEADS // 2)
            sp.wait_ge(v_out[1], 16 * HEADS // 2)
            sp.wait_ge(stored_sp, 2 * 16)
            sp.wait_ge(stored, 3 * 16)

        @block.gpsimd
        def _(pool):
            g = nc.gpsimd
            g.memset(ident[:, :], 0.0).then_inc(consts_ready, 1)
            g.memset(vn[:, 0:P], 1.0).then_inc(consts_ready, 1)
            g.memset(small[:, :], EPS).then_inc(consts_ready, 1)
            g.memset(zpad[:, :], 0.0).then_inc(consts_ready, 1)
            pool.wait_ge(consts_ready, 4)
            g.affine_select(out=ident[:, :], in_=ident[:, :], compare_op=ALU.not_equal, fill=1.0, base=0,
                            pattern=[[-1, P]], channel_multiplier=1).then_inc(consts_ready, 1)
            g.memset(blk_mask, 1.0).then_inc(consts_ready, 1)
            pool.wait_ge(consts_ready, 6)
            g.affine_select(out=blk_mask, in_=blk_mask, compare_op=ALU.is_ge, fill=0.0, base=0,
                            pattern=[[-NS, NB]], channel_multiplier=1).then_inc(consts_ready, 1)
            pool.wait_ge(consts_ready, 7)
            g.affine_select(out=blk_mask, in_=blk_mask, compare_op=ALU.is_ge, fill=0.0, base=NS - 1,
                            pattern=[[NS, NB]], channel_multiplier=-1).then_inc(consts_ready, 1)

            rows = ((G_FFN, norm_ffn_g[0], 16), (G_FIN, final_norm_g, 16),
                    (G_SGU, sgu_norm_g[0], 8), (G_OUT, out_norm_a_g[0], 8), (G_OUT + 8, out_norm_b_g[0], 8),
                    (MIX_B, conv_mix_b[0], 8))
            for at, v, n in rows:
                g.dma_start(vec_nat[at:at + n, :], v.rearrange("(t c) -> t c", c=P)).then_inc(vecs_landed, 16)
            g.dma_start(vec_nat[MIX_W:MIX_W + 24, :],
                        conv_mix_w[0].rearrange("k (t c) -> (k t) c", c=P)).then_inc(vecs_landed, 16)
            g.dma_start(mixst_nat[:, :],
                        state_conv_mix[0].rearrange("b k (t c) -> (b k t) c", c=P)).then_inc(vecs_landed, 16)

            for tb in range(TB + 1):
                n = P if tb < TB else SAMP
                for kq in range(2):
                    pool.wait_ge(xhi_ready, 4 * tb + kq + 1)
                    g.tensor_tensor(h_lo[:, 4 * kq:4 * kq + 4, tb * P:tb * P + n], xg_of(kq, n),
                                    h_hi[:, 4 * kq:4 * kq + 4, tb * P:tb * P + n].bitcast(F32),
                                    ALU.subtract).then_inc(xlo_pool, 1)
            pool.wait_ge(x_t, 4 * (TB + 1))
            pool.wait_ge(ssqn_ready, TB + 1)
            g.memset(acc[:, :], 0.0).then_inc(acc_done, 1)
            g.dma_start(ws_nat[:, :, :], w_s[0].rearrange("h i j -> i h j")).then_inc(late_landed, 16)
            g.dma_start(ffn_nat[:, 0:3, :], conv_ffn_w[0].rearrange("k (t c) -> t k c", c=P)).then_inc(late_landed, 16)
            g.dma_start(ffn_nat[:, 3, :], conv_ffn_b[0].rearrange("(t c) -> t c", c=P)).then_inc(late_landed, 16)
            g.dma_start(ffn_nat[:, 4:, :],
                        state_conv_ffn[0].rearrange("b k (t c) -> t (b k) c", c=P)).then_inc(late_landed, 16)
            g.dma_start(bias_b[:, :, :].rearrange("p h i -> p (h i)"),
                        b_s[0].rearrange("h i -> (h i)").rearrange("(a n) -> a n", a=1).broadcast_to([P, HEADS * P])
                        ).then_inc(late_landed, 16)

            pool.wait_ge(xT_copied, 4 * (TB + 1))
            g.dma_start(scratch, X[:, :, :].rearrange("p k t -> p (k t)")).then_inc(scratch_out, 16)

            def square_sum(k, done, count):
                pool.wait_ge(*done)
                g.tensor_tensor(psq[:, :], X[:, ds(k, 1), :].rearrange("p a t -> p (a t)"),
                                X[:, ds(k, 1), :].rearrange("p a t -> p (a t)"), ALU.mult).then_inc(acc_done, 1)
                pool.wait_ge(acc_done, count + 1)
                g.tensor_tensor(acc[:, :], acc[:, :], psq[:, :], ALU.add).then_inc(acc_done, 1)
                pool.wait_ge(acc_done, count + 2)

            pool.wait_ge(acc_done, 1)
            for i in range(2):
                square_sum(i, (gelu_done, i + 1), 2 * i + 1)
            pool.wait_ge(param_ready, 2)
            g.affine_select(out=wsT[:, :, :], in_=wsT[:, :, :], compare_op=ALU.is_ge, fill=0.0, base=0,
                            pattern=[[0, HEADS], [1, P]], channel_multiplier=-1).then_inc(ws_masked, 1)
            with pool.Fori(2, HEADS) as i:
                square_sum(i, (gelu_done, i + 1), i * 2 + 1)
            vc = new_chunk_v[0].rearrange("b s c -> (b s) c")
            with pool.Fori(0, HEADS // 2) as i:
                for s in range(2):
                    pool.wait_ge(v_ready, i * 2 + (s + 1))
                    g.dma_start(vc[:, ds(i * (2 * P) + s * P, P)], v_nat[0:SAMP, s, TB, :]).then_inc(v_out[s], 16)

            def conv_pads(k, src):
                pool.wait_ge(conv_done, k)
                g.tensor_copy(zs[:, :, 0:2], src).then_inc(pads_ready, 1)

            def save_rows(k, dst, i):
                pool.wait_ge(z_ready, k + 1)
                g.tensor_copy(dst[:, 0:2, ds(i, 1)].rearrange("p r a -> p (r a)"), zpad[:, SEQ:SEQ + 2])
                g.tensor_copy(dst[:, 2:, ds(i, 1)].rearrange("p (b k) a -> p b (k a)", b=NB),
                              zs[:, :, NS:NS + 2]).then_inc(rows_saved, 1)

            def mix_state(i):
                return mixst[:, :, ds(i, 1)].rearrange("p (b k) a -> p b (k a)", b=NB)

            def ffn_state(f):
                return ffnv[:, 4:, ds(f, 1)].rearrange("p (b k) a -> p b (k a)", b=NB)

            pool.wait_ge(vec_ready, 3)
            g.tensor_copy(zs[:, :, 0:2], mix_state(0)).then_inc(pads_ready, 1)
            save_rows(0, mix_rows, 0)
            with pool.Fori(1, HEADS) as i:
                conv_pads(i, mix_state(i))
                save_rows(i, mix_rows, i)
            for s in range(4):
                pool.wait_ge(ylo_ready, 4 * s + 4)
                g.dma_start(X[:, 4 * s:4 * s + 4, :].rearrange("p k t -> p (k t)"),
                            scratch[:, 4 * s * T:(4 * s + 4) * T]).then_inc(resid_in, 16)
            pool.wait_ge(ssq_done, KT + 2)
            g.memset(acc[:, :], 0.0).then_inc(acc_done, 1)
            pool.wait_ge(acc_done, 2 * HEADS + 2)
            with pool.Fori(0, KT) as m:
                square_sum(m, (tile_read, m + (IN_TILES + 1)), m * 2 + (2 * HEADS + 2))
            with pool.Fori(0, FT) as f:
                conv_pads(f + HEADS, ffn_state(f))
                save_rows(f + HEADS, ffn_rows, f)
            pool.wait_ge(rms_ready, 3 + KT)
            g.memset(acc[:, :], 0.0).then_inc(facc_done, 1)
            pool.wait_ge(rows_staged, 1)
            g.dma_start(new_ffn_prompt[0, 0].rearrange("r (t c) -> t r c", c=P), ffn_stage[:, 0:2, :]).then_inc(rows_out, 16)
            g.dma_start(new_ffn_sample[0].rearrange("b k (t c) -> t (b k) c", c=P), ffn_stage[:, 2:, :]).then_inc(rows_out, 16)
            g.dma_start(new_mix_prompt[0, 0].rearrange("r (t c) -> (r t) c", c=P), mix_stage[0:16, 0, :]).then_inc(rows_out, 16)
            g.dma_start(new_mix_sample[0].rearrange("b k (t c) -> (b k t) c", c=P), mix_stage[:, 1, :]).then_inc(rows_out, 16)
            pool.wait_ge(facc_done, 1)
            with pool.Fori(0, KT // 2) as j:
                for s in range(2):
                    pool.wait_ge(fsq_ready, j * 2 + (s + 1))
                    g.tensor_tensor(acc[:, :], acc[:, :], fin_sq[s][:, :], ALU.add).then_inc(facc_done, 1)
                    pool.wait_ge(facc_done, j * 2 + (s + 2))
            for n, tb in enumerate((0, 2, 4)):
                pool.wait_ge(out_d, n + 1)
                if tb < TB:
                    g.dma_start(y_prompt[0][tb * P:(tb + 1) * P, :], out_nat[:, tb, :]).then_inc(stored, 16)
                else:
                    g.dma_start(y_sample.rearrange("b s d -> (b s) d"), out_nat[0:SAMP, tb, :]).then_inc(stored, 16)

        @block.scalar
        def _(act):
            a = nc.scalar

            def split_hi(q, c, free=None):
                if free is not None:
                    act.wait_ge(*free)
                act.wait_ge(raw_landed[c % 2], landed(q, c))
                a.activation(w_hi[:, c % 4], raw[:, c % 2], ACT.Copy).then_inc(hi_ready, 1)

            def landed(q, c):
                return (q - c % 2) * 8 + 16

            def root(n, scale, prev):
                act.wait_ge(ssq_done, n)
                if prev is not None:
                    act.wait_ge(*prev)
                a.activation(rms[:, 0:SEQ], ps[:, SSQ_BANK, :], ACT.Sqrt, bias=eps_t, scale=scale)
                a.activation(rms[:, SEQ:T], ssq_samp, ACT.Sqrt, bias=eps_t, scale=scale).then_inc(rms_ready, 1)

            act.wait_ge(vec_t, 1)
            a.activation(vecs[:, 0:KT], ps[:, 1, 0:KT], ACT.Copy).then_inc(vec_ready, 1)
            def x_hi(u):
                tb, kq = u // 4, u % 4
                n = P if tb < TB else SAMP
                act.wait_ge(xg_ready, u + 1)
                a.activation(h_hi[:, 4 * kq:4 * kq + 4, tb * P:tb * P + n], xg_of(kq, n),
                             ACT.Copy).then_inc(xhi_ready, 1)

            for tb in range(TB + 1):
                n = P if tb < TB else SAMP
                for kq in range(4):
                    u = 4 * tb + kq
                    act.wait_ge(x_t, u + 1)
                    a.activation(X[:, 4 * kq:4 * kq + 4, tb * P:tb * P + n],
                                 ps[:, 4 + kq, 0:4 * n].rearrange("p (k t) -> p k t", k=4),
                                 ACT.Copy).then_inc(xT_copied, 1)
                    if u >= 1:
                        x_hi(u - 1)
                if tb == 1:
                    for c in range(2):
                        split_hi(c, c)
            x_hi(4 * TB + 3)
            act.wait_ge(vec_t, 2)
            a.activation(vecs[:, KT:], ps[:, 2, KT:104], ACT.Copy).then_inc(vec_ready, 1)
            a.activation(mixst[:, :, :].rearrange("p r t -> p (r t)"), ps[:, 2, 128:256],
                         ACT.Copy).then_inc(vec_ready, 1)
            act.wait_ge(xT_copied, 4 * (TB + 1))
            for order, tb in enumerate((TB, *range(TB))):
                n = P if tb < TB else SAMP
                if order >= 1:
                    act.wait_ge(ssqn_ready, order)
                a.activation(ps[0:n, 4:8, :].rearrange("p a b -> p (a b)"), x_nat[tb][0:n, :], ACT.Square,
                             accum_out=ssq_nat[0:n, tb:tb + 1]).then_inc(ssqn_ready, 1)
                if order == 1:
                    for c in range(2, 4):
                        split_hi(c, c)
            root(1, 1.0 / DM, None)

            def gelu_v(i, t):
                act.wait_ge(tile_read, t + 1)
                a.activation(X[:, ds(i, 1), :].rearrange("p a t -> p (a t)"), scaled[:, :],
                             ACT.Gelu_apprx_tanh).then_inc(gelu_done, 1)

            def split2_hi(q, c, done):
                for s in range(2):
                    split_hi(q + s, c + s, (piece_done, done + s))

            def split4_hi(q, only=range(4)):
                for c in only:
                    split_hi(q + 4 + c, c, (piece_done, q + (1, 3, 2, 4)[c]))

            split2_hi(4, 0, 1)
            act.wait_ge(scratch_out, 16)
            gelu_v(0, 0)
            gelu_v(1, 1)
            split2_hi(6, 2, 3)
            act.wait_ge(param_t, 1)
            for n in range(2):
                a.activation(wsT[:, 4 * n:4 * n + 4, :].rearrange("p h i -> p (h i)"), ps[:, 4 + n, :],
                             ACT.Copy).then_inc(param_ready, 1)
            a.activation(ffnv[:, 0:11, :].rearrange("p r t -> p (r t)"), ps[:, 6, 0:11 * FT],
                         ACT.Copy).then_inc(param_ready, 1)
            a.activation(ffnv[:, 11:, :].rearrange("p r t -> p (r t)"), ps[:, 7, 0:9 * FT],
                         ACT.Copy).then_inc(param_ready, 1)
            with act.Fori(1, HEADS // 2) as i:
                for s in range(2):
                    gelu_v(i * 2 + s, i * 2 + s)
                    split2_hi(i * 4 + (2 * s + 4), 2 * s, i * 4 + (2 * s + 1))

            def gelu_u(i):
                act.wait_ge(tile_read, i + (HEADS + 1))
                a.activation(u_gelu[:, :], scaled[:, :], ACT.Gelu_apprx_tanh).then_inc(gelu_done, 1)

            def v_store(i, s):
                act.wait_ge(v_t, i + 1)
                a.activation(v_nat[:, s, 0:TB, :].rearrange("p b d -> p (b d)"), ps[:, T_BANK, :], ACT.Copy)
                a.activation(v_nat[0:SAMP, s, TB, :], t_samp, ACT.Copy).then_inc(v_ready, 1)

            root(2, 1.0 / AW, (rrms_ready, 1))
            gelu_u(0)
            v_store(0, 0)
            split2_hi(2 * HEADS + 4, 0, 2 * HEADS + 1)
            act.wait_ge(y_raw, 1)
            gelu_u(1)
            v_store(1, 1)
            root(3, 1.0 / P, (rrms_ready, 2))
            split2_hi(2 * HEADS + 6, 2, 2 * HEADS + 3)
            with act.Fori(1, HEADS // 2) as i:
                for s in range(2):
                    n = i * 2 + (s + 1)
                    act.wait_ge(mix_done, n - 2)
                    act.wait_ge(v_out[s], i * 16)
                    v_store(n - 1, s)
                    act.wait_ge(y_raw, n - 1)
                    gelu_u(n - 1)
                    root(n + 1, 1.0 / P, (y_ready, n - 2))
                    split2_hi(i * 4 + (2 * HEADS + 4 + 2 * s), 2 * s, i * 4 + (2 * HEADS + 1 + 2 * s))

            def tap2(k, w, b, prev):
                act.wait_ge(z_ready, k + 1)
                act.wait_ge(pads_ready, k + 1)
                if prev is not None:
                    act.wait_ge(*prev)
                a.activation(cv[:, :], zpad[:, 2:ZP], ACT.Identity, bias=b, scale=w).then_inc(tap2_done, 1)

            def group_b(i, c, first=False, last=False):
                q = i * 6 + 4 * HEADS
                root(i + (HEADS + 2), 1.0 / P, (y_ready, i + (HEADS - 1)))
                split2_hi(q + 4, c, q + 1)
                tap2(i, vecs[:, ds(i + (MIX_W + 16), 1)], vecs[:, ds(i + MIX_B, 1)],
                     None if first else (y_raw, i + HEADS))
                split2_hi(q + 6, c + 2, q + 3)
                if last:
                    split_hi(q + 8, c, (piece_done, q + 5))
                else:
                    split2_hi(q + 8, c, q + 5)

            group_b(0, 0, first=True)
            group_b(1, 2)
            with act.Fori(1, HEADS // 2 - 1) as i:
                group_b(i * 2, 0)
                group_b(i * 2 + 1, 2)
            group_b(HEADS - 2, 0)
            group_b(HEADS - 1, 2, last=True)

            def y_hi(k):
                act.wait_ge(y_ready, k + 1)
                a.activation(h_hi[:, ds(k, 1), :].rearrange("p a t -> p (a t)"),
                             X[:, ds(k, 1), :].rearrange("p a t -> p (a t)"), ACT.Copy).then_inc(yhi_ready, 1)

            act.wait_ge(piece_done, IN_PIECES)
            with act.Fori(0, PK) as k:
                y_hi(k)
            split_hi(IN_PIECES + 3, 3)
            root(2 + KT, 1.0 / P, (y_ready, KT - 1))
            with act.Fori(PK, KT) as k:
                y_hi(k)
            split4_hi(IN_PIECES)
            with act.Fori(1, KT // 2 - 1) as i:
                for s in range(2):
                    split2_hi(i * 4 + (IN_PIECES + 4 + 2 * s), 2 * s, i * 4 + (IN_PIECES + 1 + 2 * s))
            split2_hi(GEMM_PIECES, 0, GEMM_PIECES - 3)
            split_hi(GEMM_PIECES + 2, 2, (piece_done, GEMM_PIECES - 1))
            act.wait_ge(piece_done, GEMM_PIECES)

            def h_hi_k(k):
                act.wait_ge(tile_read, k + (IN_TILES + 1))
                a.activation(h_hi[:, ds(k, 1), :].rearrange("p a t -> p (a t)"),
                             X[:, ds(k, 1), :].rearrange("p a t -> p (a t)"), ACT.Copy,
                             scale=vecs[:, ds(k + G_FFN, 1)]).then_inc(hhi_ready, 1)

            with act.Fori(0, PK) as k:
                h_hi_k(k)
            split_hi(GEMM_PIECES + 3, 3)
            with act.Fori(PK, KT) as k:
                h_hi_k(k)
            root(3 + KT, 1.0 / DM, (y_ready, KT))
            split4_hi(GEMM_PIECES, range(1))

            def gate(f, q, c, done, first=False):
                tap2(f + HEADS, ffnv[:, 2, ds(f, 1)], ffnv[:, 3, ds(f, 1)], None)
                if first:
                    split4_hi(GEMM_PIECES, range(1, 2))
                else:
                    split2_hi(q, c, done)
                act.wait_ge(conv_done, f + (HEADS + 1))
                if not first:
                    act.wait_ge(act_prod, f)
                a.activation(gate_act[:, :], cv[:, :], ACT.Silu).then_inc(silu_done, 1)

            def up(f, s):
                act.wait_ge(act_prod, f + 1)
                a.activation(act_hi[:, s, :], prod[:, :], ACT.Copy).then_inc(acthi_ready, 1)

            gate(0, GEMM_PIECES + 4, 0, GEMM_PIECES + 1, first=True)
            up(0, 0)
            split4_hi(GEMM_PIECES, range(2, 4))
            gate(1, blk_q(1), 0, GEMM_PIECES + 5)
            up(1, 1)
            split2_hi(blk_q(1) + 2, 2, GEMM_PIECES + 7)
            def states_out():
                act.wait_ge(rows_t, 1)
                flat = ffn_stage[:, :, :].rearrange("t r c -> t (r c)")
                for n in range(5):
                    m = min(512, ROWS * P - 512 * n)
                    a.activation(flat[:, 512 * n:512 * n + m], ps[0:FT, n, 0:m], ACT.Copy)
                a.activation(mix_stage[0:16, 0, :], ps[0:16, 4, 256:384], ACT.Copy)
                a.activation(mix_stage[:, 1, :], ps[:, 4, 384:512], ACT.Copy).then_inc(rows_staged, 1)

            def ffn_block(b, last=False):
                q, p, d = blk_q(b), blk_p(b), (b - 1) * 16
                gate(b * 2, q + 4, 0, p + 1)
                for c in range(4):
                    split_hi(q + 6 + c, 2 + c, (down_done, d + 4 * (c + 1)))
                up(b * 2, 0)
                split2_hi(q + 10, 2, p + 3)
                gate(b * 2 + 1, blk_q(b + 1), 0, p + 5)
                if last:
                    states_out()
                up(b * 2 + 1, 1)
                split2_hi(blk_q(b + 1) + 2, 2, p + 7)

            with act.Fori(1, NBLK - 1) as b:
                ffn_block(b)
            ffn_block(NBLK - 1, last=True)
            D0 = (NBLK - 1) * 16

            def last_tile(j, s, first):
                act.wait_ge(down_added, j + (D0 + 1))
                xj = X[:, ds(j, 1), :].rearrange("p a t -> p (a t)")
                if not first:
                    act.wait_ge(facc_done, j)
                a.activation(fin_sq[s][:, :], xj, ACT.Square).then_inc(fsq_ready, 1)
                if not first:
                    act.wait_ge(f_t, j - 1)
                a.activation(fin_g[s][:, :], xj, ACT.Copy, scale=vecs[:, ds(j + G_FIN, 1)]).then_inc(fg_ready, 1)

            for s in range(2):
                last_tile(s, s, True)
            with act.Fori(1, KT // 2) as i:
                for s in range(2):
                    last_tile(i * 2 + s, s, False)
            act.wait_ge(fssq_done, 1)
            a.activation(rms_nat[:, 0:TB], ps[:, 0, 0:TB], ACT.Sqrt, bias=eps_t, scale=1.0 / DM)
            a.activation(rms_nat[0:SAMP, TB:TB + 1], ps[0:SAMP, 0, TB:TB + 1], ACT.Sqrt, bias=eps_t[0:SAMP],
                         scale=1.0 / DM).then_inc(frms_ready, 1)
            act.wait_ge(frrms_ready, 1)
            act.wait_ge(f_ready, KT)
            for tb in (1, 3):
                a.activation(out_nat[:, tb, :], out_nat[:, tb, :], ACT.Copy,
                             scale=rms_nat[:, tb:tb + 1]).then_inc(out_a, 1)

        @block.vector
        def _(dve):
            v = nc.vector

            def row(buf, k):
                return buf[:, ds(k, 1), :].rearrange("p a t -> p (a t)")

            def split_lo(q, c):
                dve.wait_ge(hi_ready, q + 1)
                v.tensor_tensor(w_lo[:, c % 4], raw[:, c % 2], w_hi[:, c % 4].bitcast(F32),
                                ALU.subtract).then_inc(lo_ready, 1)

            def split2_lo(q, c):
                for s in range(2):
                    split_lo(q + s, c + s)

            def times_rb(dst, p, done):
                v.tensor_tensor(dst[:, 0:HALF], pair(p, 0), rb[:, 0:HALF], ALU.mult)
                v.tensor_tensor(dst[:, HALF:T], pair(p, 1), rb[:, HALF:T], ALU.mult).then_inc(done, 1)

            def reciprocal_rms(n, dst):
                dve.wait_ge(rms_ready, n)
                v.reciprocal(dst[:, :], rms[:, :]).then_inc(rrms_ready, 1)

            dve.wait_ge(consts_ready, 2)
            v.tensor_copy(ones_r[:, :], vn[:, 0:P]).then_inc(ones_ready, 1)

            def x_lo(u):
                tb, kq = u // 4, u % 4
                n = P if tb < TB else SAMP
                at = (slice(None), slice(4 * kq, 4 * kq + 4), slice(tb * P, tb * P + n))
                dve.wait_ge(xhi_ready, u + 1)
                v.tensor_tensor(h_lo[at], xg_of(kq, n), h_hi[at].bitcast(F32), ALU.subtract).then_inc(xlo_dve, 1)

            dve.wait_ge(vec_ready, 1)
            for tb in range(TB + 1):
                n = P if tb < TB else SAMP
                for kq in range(4):
                    u = 4 * tb + kq
                    dve.wait_ge(xT_copied, u + 1)
                    if tb >= 1:
                        if kq < 2:
                            dve.wait_ge(xlo_pool, 2 * (tb - 1) + kq + 1)
                        elif kq == 2:
                            x_lo(u - 4)
                            x_lo(u - 3)
                            dve.wait_ge(xlo_dve, 2 * tb)
                    gain = vecs[:, G_MIX + 4 * kq:G_MIX + 4 * kq + 4].rearrange("p (k a) -> p k a", a=1).broadcast_to([P, 4, n])
                    v.tensor_tensor(xg_of(kq, n), X[:, 4 * kq:4 * kq + 4, tb * P:tb * P + n], gain,
                                    ALU.mult).then_inc(xg_ready, 1)
                if tb == 1:
                    split2_lo(0, 0)
            for u in (4 * TB + 2, 4 * TB + 3):
                x_lo(u)
            split2_lo(2, 2)
            dve.wait_ge(ssqn_ready, TB + 1)
            dve.wait_ge(consts_ready, 8)
            for tb in range(TB + 1):
                n = P if tb < TB else SAMP
                d = v.tensor_scalar(sq[0:n, tb * P:tb * P + n], ident[0:n, 0:n], ssq_nat[0:n, tb:tb + 1], None, ALU.mult)
            d.then_inc(diag_ready, 1)
            v.tensor_copy(sel[:, :, :], ident[:, 0:NS].rearrange("p (a j) -> p a j", a=1).broadcast_to([P, NB, NS])
                          ).then_inc(sel_ready, 1)
            reciprocal_rms(1, rb)
            dve.wait_ge(rrms_ready, 1)
            dve.wait_ge(xlo_pool, 2 * (TB + 1))

            def v_tile(t, s, first=False):
                dve.wait_ge(piece_done, t * 2 + 2)
                if not first:
                    dve.wait_ge(gelu_done, t)
                times_rb(scaled, s, tile_read)

            for t in range(2):
                v_tile(t, t, first=t == 0)
                split2_lo(2 * t + 4, 2 * t)
            with dve.Fori(1, HEADS // 2) as i:
                for s in range(2):
                    v_tile(i * 2 + s, s)
                    split2_lo(i * 4 + (2 * s + 4), 2 * s)

            dve.wait_ge(corner_done, 1)
            v.tensor_tensor(ws_blk[:, :, :, :],
                            ps[0:SAMP, 4, 0:SAMP].rearrange("p (h a i) -> p h a i", h=HEADS, a=1).broadcast_to([SAMP, HEADS, NB, NS]),
                            blk_mask.rearrange("p (a b c) -> p a b c", a=1, c=1).broadcast_to([SAMP, HEADS, NB, NS]),
                            ALU.mult).then_inc(blk_ready, 1)

            def norm_v(i):
                v.scalar_tensor_tensor(out=vn[:, :], in0=row(X, i), scalar=vecs[:, ds(i + G_SGU, 1)],
                                       in1=rv[:, :], op0=ALU.mult, op1=ALU.mult).then_inc(vn_ready, 1)

            def square_y(n):
                dve.wait_ge(y_raw, n + 1)
                dve.wait_ge(ssq_done, n + 2)
                v.tensor_tensor(sq[:, :], row(X, n), row(X, n), ALU.mult).then_inc(y_sq, 1)

            def split_square(n):
                dve.wait_ge(y_sq, n * 3 + 1)
                v.tensor_copy(sq_hi[:, :], sq[:, :]).then_inc(y_sq, 1)
                dve.wait_ge(y_sq, n * 3 + 2)
                v.tensor_tensor(sq_lo[:, :], sq[:, :], sq_hi[:, :].bitcast(F32), ALU.subtract).then_inc(y_sq, 1)

            def norm_y(n):
                reciprocal_rms_inplace(n)
                v.scalar_tensor_tensor(out=row(X, n), in0=row(X, n), scalar=vecs[:, ds(n + G_OUT, 1)],
                                       in1=rms[:, :], op0=ALU.mult, op1=ALU.mult).then_inc(y_ready, 1)

            def reciprocal_rms_inplace(n):
                reciprocal_rms(n + 3, rms)
                dve.wait_ge(rrms_ready, n + 3)

            def gate_a(i):
                dve.wait_ge(mix_done, i + 1)
                bi = bias_b[:, ds(i, 1), :]
                v.tensor_tensor(prod[:, 0:SEQ].rearrange("p (c t) -> p c t", c=TB),
                                ps[:, MIX_BANK, :].rearrange("p (c t) -> p c t", c=TB),
                                bi.broadcast_to([P, TB, P]), ALU.add)
                v.tensor_tensor(samp8(prod[:, SEQ:T]), samp8(mix_samp),
                                bias_b[:, ds(i, 1), 0:NS].broadcast_to([P, NB, NS]), ALU.add).then_inc(mix_read, 1)
                dve.wait_ge(mix_read, i + 1)
                dve.wait_ge(gelu_done, i + (HEADS + 1))
                v.tensor_tensor(row(X, i), prod[:, :], u_gelu[:, :], ALU.mult).then_inc(y_raw, 1)
                square_y(i)

            dve.wait_ge(rms_ready, 2)
            v.reciprocal(rv[:, :], rms[:, :]).then_inc(rrms_ready, 1)
            dve.wait_ge(rrms_ready, 2)
            dve.wait_ge(ones_ready, 1)
            dve.wait_ge(late_landed, 5 * 16)
            norm_v(0)

            def u_tile(i, s):
                dve.wait_ge(piece_done, i * 2 + (2 * HEADS + 2))
                dve.wait_ge(gelu_done, i + HEADS)
                times_rb(scaled, s, tile_read)

            u_tile(0, 0)
            split2_lo(2 * HEADS + 4, 0)
            dve.wait_ge(v_t, 1)
            norm_v(1)
            gate_a(0)
            u_tile(1, 1)
            split_square(0)
            split2_lo(2 * HEADS + 6, 2)
            dve.wait_ge(v_t, 2)
            norm_v(2)
            norm_y(0)
            gate_a(1)
            with dve.Fori(1, HEADS // 2 - 1) as i:
                for s in range(2):
                    n = i * 2 + (s + 1)
                    u_tile(n - 1, s)
                    split_square(n - 2)
                    split2_lo(i * 4 + (2 * HEADS + 4 + 2 * s), 2 * s)
                    dve.wait_ge(v_t, n)
                    norm_v(n)
                    norm_y(n - 2)
                    gate_a(n - 1)
            u_tile(HEADS - 2, 0)
            split_square(HEADS - 3)
            split2_lo(4 * HEADS, 0)
            dve.wait_ge(v_t, HEADS - 1)
            norm_v(HEADS - 1)
            norm_y(HEADS - 3)
            gate_a(HEADS - 2)
            u_tile(HEADS - 1, 1)
            split_square(HEADS - 2)
            split2_lo(4 * HEADS + 2, 2)
            norm_y(HEADS - 2)
            gate_a(HEADS - 1)
            split_square(HEADS - 1)

            def conv_taps(k, w1, w0):
                dve.wait_ge(tap2_done, k + 1)
                v.scalar_tensor_tensor(out=cv[:, :], in0=zpad[:, 1:ZP - 1], scalar=w1, in1=cv[:, :],
                                       op0=ALU.mult, op1=ALU.add).then_inc(tap1_done, 1)
                dve.wait_ge(tap1_done, k + 1)
                v.scalar_tensor_tensor(out=cv[:, :], in0=zpad[:, 0:ZP - 2], scalar=w0, in1=cv[:, :],
                                       op0=ALU.mult, op1=ALU.add).then_inc(conv_done, 1)

            def y_lo(k):
                dve.wait_ge(yhi_ready, k + 1)
                v.tensor_tensor(row(h_lo, k), row(X, k), row(h_hi, k).bitcast(F32), ALU.subtract).then_inc(ylo_ready, 1)

            def group_b(i, first, c, last=False):
                t = i * 3 + 2 * HEADS
                q = t * 2
                dve.wait_ge(piece_done, q + 2)
                if first:
                    dve.wait_ge(gelu_done, 2 * HEADS)
                times_rb(scaled, (c // 2) % 2, tile_read)
                split2_lo(q + 4, c)
                norm_y(i + (HEADS - 1))
                dve.wait_ge(piece_done, q + 4)
                times_rb(prod, (c // 2 + 1) % 2, tile_read)
                dve.wait_ge(tile_read, t + 2)
                if first:
                    dve.wait_ge(pads_ready, 1)
                else:
                    dve.wait_ge(rows_saved, i)
                v.tensor_tensor(zpad[:, 2:2 + SEQ], prod[:, 0:SEQ], scaled[:, 0:SEQ], ALU.mult)
                v.tensor_tensor(zs[:, :, 2:], samp8(prod[:, SEQ:T]), samp8(scaled[:, SEQ:T]),
                                ALU.mult).then_inc(z_ready, 1)
                split2_lo(q + 6, c + 2)
                conv_taps(i, vecs[:, ds(i + (MIX_W + 8), 1)], vecs[:, ds(i + MIX_W, 1)])
                if last:
                    split_lo(q + 8, c)
                dve.wait_ge(piece_done, q + 6)
                dve.wait_ge(z_ready, i + 1)
                times_rb(prod, (c // 2) % 2, tile_read)
                dve.wait_ge(tile_read, t + 3)
                dve.wait_ge(conv_done, i + 1)
                if last:
                    for k in range(2):
                        y_lo(k)
                yi = X[:, ds(i + HEADS, 1), :].rearrange("p a t -> p (a t)")
                v.tensor_tensor(yi[:, 0:SEQ], prod[:, 0:SEQ], cv[:, 0:SEQ], ALU.mult)
                v.tensor_tensor(samp8(yi[:, SEQ:T]), samp8(prod[:, SEQ:T]), conv_samp(cv), ALU.mult).then_inc(y_raw, 1)
                square_y(i + HEADS)
                split_square(i + HEADS)
                if not last:
                    split2_lo(q + 8, c)

            group_b(0, True, 0)
            group_b(1, False, 2)
            with dve.Fori(1, HEADS // 2 - 1) as i:
                group_b(i * 2, False, 0)
                group_b(i * 2 + 1, False, 2)
            group_b(HEADS - 2, False, 0)
            group_b(HEADS - 1, False, 2, last=True)

            with dve.Fori(2, PK) as k:
                y_lo(k)
            split_lo(IN_PIECES + 3, 3)
            for k in range(PK, PK + 2):
                y_lo(k)
            norm_y(KT - 1)
            with dve.Fori(PK + 2, KT) as k:
                y_lo(k)

            def w_out_tile(m, s, done=None):
                dve.wait_ge(piece_done, m * 2 + (IN_PIECES + 2) if done is None else done)
                xm = row(X, m)
                v.tensor_tensor(xm[:, 0:HALF], xm[:, 0:HALF], pair(s, 0), ALU.add)
                v.tensor_tensor(xm[:, HALF:T], xm[:, HALF:T], pair(s, 1), ALU.add).then_inc(tile_read, 1)

            split_lo(IN_PIECES + 4, 0)
            dve.wait_ge(resid_in, 4 * 16)
            w_out_tile(0, 0, IN_PIECES + 3)
            split_lo(IN_PIECES + 5, 1)
            w_out_tile(1, 1)
            split2_lo(IN_PIECES + 6, 2)
            with dve.Fori(1, KT // 2 - 1) as i:
                for s in range(2):
                    split2_lo(i * 4 + (IN_PIECES + 4 + 2 * s), 2 * s)
                    w_out_tile(i * 2 + s, s)
            split2_lo(GEMM_PIECES, 0)
            w_out_tile(KT - 2, 0)
            split_lo(GEMM_PIECES + 2, 2)
            w_out_tile(KT - 1, 1)

            def h_lo_k(k):
                dve.wait_ge(hhi_ready, k + 1)
                v.scalar_tensor_tensor(out=row(h_lo, k), in0=row(X, k), scalar=vecs[:, ds(k + G_FFN, 1)],
                                       in1=row(h_hi, k).bitcast(F32), op0=ALU.mult,
                                       op1=ALU.subtract).then_inc(hlo_ready, 1)

            with dve.Fori(0, PK) as k:
                h_lo_k(k)
            split_lo(GEMM_PIECES + 3, 3)
            with dve.Fori(PK, KT) as k:
                h_lo_k(k)
            reciprocal_rms(3 + KT, rb)
            dve.wait_ge(rrms_ready, 3 + KT)

            def gate_in(f, p, done):
                dve.wait_ge(piece_done, done)
                dve.wait_ge(rows_saved, f + HEADS)
                n = SEQ - HALF
                v.tensor_tensor(zpad[:, 2:2 + HALF], pair(p, 0), rb[:, 0:HALF], ALU.mult)
                v.tensor_tensor(zpad[:, 2 + HALF:2 + SEQ], ps[:, 2 * p + 1, 0:n], rb[:, HALF:SEQ], ALU.mult)
                v.tensor_tensor(zs[:, :, 2:], samp8(ps[:, 2 * p + 1, n:HALF]), samp8(rb[:, SEQ:T]),
                                ALU.mult).then_inc(z_ready, 1)

            def gate_conv(f):
                conv_taps(f + HEADS, ffnv[:, 1, ds(f, 1)], ffnv[:, 0, ds(f, 1)])

            def up_in(f, p, done, s, first=False):
                dve.wait_ge(piece_done, done)
                if not first:
                    dve.wait_ge(act_ready, f)
                times_rb(scaled, p, up_read)
                dve.wait_ge(up_read, f + 1)
                dve.wait_ge(silu_done, f + 1)
                v.tensor_tensor(prod[:, 0:SEQ], scaled[:, 0:SEQ], gate_act[:, 0:SEQ], ALU.mult)
                v.tensor_tensor(samp8(prod[:, SEQ:T]), samp8(scaled[:, SEQ:T]), conv_samp(gate_act),
                                ALU.mult).then_inc(act_prod, 1)
                dve.wait_ge(acthi_ready, f + 1)
                v.tensor_tensor(act_lo[:, s, :], prod[:, :], act_hi[:, s, :].bitcast(F32),
                                ALU.subtract).then_inc(act_ready, 1)

            def down_add(j, p, done):
                dve.wait_ge(down_done, done)
                v.tensor_tensor(X[:, j, 0:HALF], X[:, j, 0:HALF], pair(p, 0), ALU.add)
                v.tensor_tensor(X[:, j, HALF:T], X[:, j, HALF:T], pair(p, 1), ALU.add).then_inc(down_added, 1)

            g0 = GEMM_PIECES
            split_lo(g0 + 4, 0)
            gate_in(0, 0, g0 + 3)
            split_lo(g0 + 5, 1)
            gate_conv(0)
            up_in(0, 1, g0 + 4, 0, first=True)
            split2_lo(g0 + 6, 2)
            gate_in(1, 2, g0 + 6)
            split2_lo(blk_q(1), 0)
            gate_conv(1)
            up_in(1, 3, g0 + 8, 1)
            split2_lo(blk_q(1) + 2, 2)
            with dve.Fori(1, NBLK) as b:
                q, p, d = blk_q(b), blk_p(b), (b - 1) * 16
                gate_in(b * 2, 0, p + 2)
                for j in range(16):
                    if j in (0, 2):
                        split_lo(q + 4 + j // 2, j // 2)
                    down_add(j, (j + 1) % 4, d + (j + 1))
                    if j == 3:
                        gate_conv(b * 2)
                    if j in (6, 10, 13):
                        split_lo(q + 6 + (6, 10, 13).index(j), 2 + (6, 10, 13).index(j))
                split_lo(q + 9, 5)
                up_in(b * 2, 1, p + 4, 0)
                split2_lo(q + 10, 2)
                gate_in(b * 2 + 1, 2, p + 6)
                split2_lo(blk_q(b + 1), 0)
                gate_conv(b * 2 + 1)
                up_in(b * 2 + 1, 3, p + 8, 1)
                split2_lo(blk_q(b + 1) + 2, 2)

            D0 = (NBLK - 1) * 16
            dve.wait_ge(piece_done, blk_p(NBLK))

            def out_store(j, s):
                dve.wait_ge(f_t, j + 1)
                v.tensor_copy(out_nat[:, 0:TB, j * P:(j + 1) * P],
                              ps[:, 4 + 2 * s, :].rearrange("p (b c) -> p b c", b=TB))
                v.tensor_copy(out_nat[0:SAMP, TB, j * P:(j + 1) * P], ps[0:SAMP, 5 + 2 * s, 0:P]).then_inc(f_ready, 1)

            for j in range(16):
                down_add(j, j if j < 4 else j % 2, D0 + j + 1)
                if j in (4, 5):
                    out_store(2 * (j - 4), 0)
                    out_store(2 * (j - 4) + 1, 1)
                elif j >= 6:
                    out_store(j - 2, j % 2)
            out_store(14, 0)
            out_store(15, 1)
            dve.wait_ge(frms_ready, 1)
            v.reciprocal(rms_nat[:, 0:TB], rms_nat[:, 0:TB])
            v.reciprocal(rms_nat[0:SAMP, TB:TB + 1], rms_nat[0:SAMP, TB:TB + 1]).then_inc(frrms_ready, 1)
            dve.wait_ge(frrms_ready, 1)
            dve.wait_ge(f_ready, KT)
            for tb in (0, 2, 4):
                n = P if tb < TB else SAMP
                v.tensor_scalar(out_nat[0:n, tb, :], out_nat[0:n, tb, :], rms_nat[0:n, tb:tb + 1], None,
                                ALU.mult).then_inc(out_d, 1)

        @block.tensor
        def _(pe):
            te = nc.tensor

            def three(out, whi, wlo, xhi, xlo, start, stop):
                te.matmul(out, whi, xhi, start=start, stop=False)
                te.matmul(out, whi, xlo, start=False, stop=False)
                return te.matmul(out, wlo, xhi, start=False, stop=stop)

            def gemm(q, c, p, q1=None, mid=None, q3=None):
                for half in range(2):
                    cols = slice(half * HALF, (half + 1) * HALF)
                    for s in range(2):
                        if half == 0:
                            pe.wait_ge(lo_ready, q + s + 1)
                        for k in range(PK):
                            kk = s * PK + k
                            last = three(pair(p, half), w_hi[:, (c + s) % 4, k, :], w_lo[:, (c + s) % 4, k, :],
                                         h_hi[:, kk, cols], h_lo[:, kk, cols], kk == 0, kk == KT - 1)
                        if half == 1:
                            last.then_inc(piece_done, 1)
                        hook = (q1, mid, q3, None)[2 * half + s]
                        if hook is not None:
                            hook()

            def gemm2_by_k(q, ready, after):
                for kk in range(KT):
                    s, k = kk // PK, kk % PK
                    pe.wait_ge(ready, kk + 1)
                    for tile in range(2):
                        c = 2 * tile + s
                        if k == 0:
                            pe.wait_ge(lo_ready, q + c + 1)
                        for half in range(2):
                            cols = slice(half * HALF, (half + 1) * HALF)
                            last = three(pair(tile, half), w_hi[:, c, k, :], w_lo[:, c, k, :],
                                         h_hi[:, kk, cols], h_lo[:, kk, cols], kk == 0, kk == KT - 1)
                        if k == PK - 1:
                            last.then_inc(piece_done, 1)
                    if kk in after:
                        after[kk]()

            def ssq(src):
                te.matmul(ps[:, SSQ_BANK, :], ones[:, :], src[:, 0:SEQ], start=True, stop=True)
                te.matmul(ssq_samp, ones[:, :], src[:, SEQ:T], start=True, stop=True).then_inc(ssq_done, 1)

            pe.wait_ge(consts_ready, 5)
            pe.wait_ge(gain_landed, 16)
            te.transpose(ps[:, 1, 0:KT], vec_nat[0:KT, :], ident[0:KT, 0:KT]).then_inc(vec_t, 1)
            for tb in range(TB + 1):
                n = P if tb < TB else SAMP
                pe.wait_ge(xnat_landed[tb], 16)
                for kq in range(4):
                    u = 4 * tb + kq
                    if tb >= 1:
                        pe.wait_ge(xT_copied, u - 3)
                    for k in range(4):
                        last = te.transpose(ps[:, 4 + kq, k * n:(k + 1) * n],
                                            x_nat[tb][0:n, (4 * kq + k) * P:(4 * kq + k + 1) * P], ident[0:n, 0:n])
                    last.then_inc(x_t, 1)
            pe.wait_ge(vecs_landed, 8 * 16)
            te.transpose(ps[:, 2, 0:104], vec_nat[0:104, :], ident[0:104, 0:104])
            te.transpose(ps[:, 2, 128:256], mixst_nat[:, :], ident[:, :]).then_inc(vec_t, 1)

            def rest_of_x():
                pe.wait_ge(xlo_pool, 2 * (TB + 1))
                pe.wait_ge(xlo_dve, 2 * (TB + 1))

            def spread_x_ssq():
                pe.wait_ge(diag_ready, 1)
                for tb in range(TB):
                    te.matmul(ps[:, SSQ_BANK, tb * P:(tb + 1) * P], ones[:, :], sq[:, tb * P:(tb + 1) * P],
                              start=True, stop=True)
                te.matmul(ssq_samp, ones[0:SAMP, :], sq[0:SAMP, SEQ:T], start=True, stop=True).then_inc(ssq_done, 1)

            def params_t():
                pe.wait_ge(late_landed, 5 * 16)
                pe.wait_ge(rms_ready, 1)
                for h in range(HEADS):
                    te.transpose(ps[:, 4 + h // 4, (h % 4) * P:(h % 4 + 1) * P], ws_nat[:, h, :], ident[:, :])
                for r in range(4 + 2 * NB):
                    b, c = (6, r) if r < 11 else (7, r - 11)
                    last = te.transpose(ps[:, b, c * FT:(c + 1) * FT], ffn_nat[:, r, :], ident[0:FT, 0:FT])
                last.then_inc(param_t, 1)

            def corner():
                pe.wait_ge(ws_masked, 1)
                pe.wait_ge(sel_ready, 1)
                pe.wait_ge(param_ready, 4)
                te.matmul(ps[0:SAMP, 4, 0:SAMP], sel[:, :, :].rearrange("p b j -> p (b j)"), wsT[:, :, 0:NS],
                          start=True, stop=True).then_inc(corner_done, 1)

            assert HALF <= 3 * P
            pe.wait_ge(xlo_pool, 2 * 3)
            pe.wait_ge(xlo_dve, 2 * 3)
            gemm(0, 0, 0, mid=rest_of_x)
            pe.wait_ge(vec_ready, 3)
            gemm(2, 2, 1, q1=spread_x_ssq, q3=params_t)
            for t in (2, 3):
                pe.wait_ge(tile_read, t - 1)
                gemm(2 * t, 2 * t, t % 2, mid=corner if t == 3 else None)
            with pe.Fori(2, HEADS // 2) as i:
                for s in range(2):
                    pe.wait_ge(tile_read, i * 2 + (s - 1))
                    gemm(i * 4 + 2 * s, 2 * s, s)

            def v_transposes(i, first=False):
                pe.wait_ge(vn_ready, i + 1)
                if not first:
                    pe.wait_ge(v_ready, i)
                    pe.wait_ge(mix_read, i)
                for b in range(TB):
                    te.transpose(ps[:, T_BANK, b * P:(b + 1) * P], vn[:, b * P:(b + 1) * P], ident[:, :])
                te.transpose(t_samp, vn[:, SEQ:T], ident[:, :]).then_inc(v_t, 1)

            def mix(i, s, roots):
                pe.wait_ge(v_ready, i + 1)
                pe.wait_ge(rms_ready, roots)
                for b in range(TB):
                    te.matmul(ps[:, MIX_BANK, b * P:(b + 1) * P], v_nat[:, s, b, :],
                              wsT[:, ds(i, 1), :].rearrange("p a i -> p (a i)"), start=True, stop=True)
                te.matmul(mix_samp, v_nat[0:SAMP, s, TB, :],
                          ws_blk[:, ds(i, 1), :, :].rearrange("p a b i -> p (a b i)"),
                          start=True, stop=True).then_inc(mix_done, 1)

            def y_ssq(n):
                pe.wait_ge(y_sq, n * 3 + 3)
                pe.wait_ge(rms_ready, n + 2)
                pe.wait_ge(ones_ready, 1)
                for cols, out in ((slice(0, SEQ), ps[:, SSQ_BANK, :]), (slice(SEQ, T), ssq_samp)):
                    te.matmul(out, ones_r[:, :], sq_hi[:, cols], start=True, stop=False)
                    last = te.matmul(out, ones_r[:, :], sq_lo[:, cols], start=False, stop=True)
                last.then_inc(ssq_done, 1)

            def v_ssq():
                pe.wait_ge(acc_done, 2 * HEADS + 1)
                ssq(acc)

            q0 = 2 * HEADS
            pe.wait_ge(tile_read, HEADS - 1)
            gemm(q0, 0, 0, mid=v_ssq)
            pe.wait_ge(tile_read, HEADS)
            pe.wait_ge(blk_ready, 1)
            v_transposes(0, first=True)
            gemm(q0 + 2, 2, 1, q3=lambda: mix(0, 0, 2))

            def step_u(i, s, q):
                pe.wait_ge(tile_read, i + (HEADS - 1))
                v_transposes(i - 1)

                def sums():
                    pe.wait_ge(v_ready, i)
                    y_ssq(i - 2)

                gemm(q, 2 * s, s, q1=sums, q3=lambda: mix(i - 1, 1 - s, i + 1))

            with pe.Fori(1, HEADS // 2) as i:
                step_u(i * 2, 0, i * 4 + q0)
                step_u(i * 2 + 1, 1, i * 4 + (q0 + 2))

            def group_b(t, q, c, mids):
                for s in range(3):
                    pe.wait_ge(tile_read, t + (s - 1))
                    gemm(q + 2 * s, c + 2 * s, (c // 2 + s) % 2, mid=mids[s])

            step_u(HEADS, 0, 4 * HEADS)
            pe.wait_ge(tile_read, 2 * HEADS)

            def last_of_a():
                pe.wait_ge(mix_read, HEADS)
                y_ssq(HEADS - 1)

            gemm(4 * HEADS + 2, 2, 1, mid=last_of_a)
            pe.wait_ge(tile_read, 2 * HEADS + 1)
            gemm(4 * HEADS + 4, 0, 0)
            group_b(2 * HEADS + 3, 4 * HEADS + 6, 2, (lambda: y_ssq(HEADS), None, None))
            with pe.Fori(1, HEADS // 2) as i:
                for s in range(2):
                    group_b(i * 6 + (2 * HEADS + 3 * s), i * 12 + (4 * HEADS + 6 * s), 2 * s,
                            (lambda: y_ssq(i * 2 + (HEADS - 1 + s)), None, None))

            pe.wait_ge(tile_read, IN_TILES)
            gemm2_by_k(IN_PIECES, ylo_ready, {1: lambda: y_ssq(KT - 1)})
            with pe.Fori(1, KT // 2) as i:
                for s in range(2):
                    pe.wait_ge(tile_read, i * 2 + (IN_TILES - 1 + s))
                    gemm(i * 4 + (IN_PIECES + 2 * s), 2 * s, s)

            def x_ssq():
                pe.wait_ge(acc_done, 2 * HEADS + 2 + 2 * KT)
                pe.wait_ge(rms_ready, KT + 2)
                ssq(acc)

            def down_tile(slot, jj, p, ks=(0, 1)):
                for half in range(2):
                    cols = slice(half * HALF, (half + 1) * HALF)
                    for k in ks:
                        last = three(pair(p, half), w_hi[:, slot, 4 * k + jj, :], w_lo[:, slot, 4 * k + jj, :],
                                     act_hi[:, k, cols], act_lo[:, k, cols], k == 0, k == 1)
                if ks[-1] == 1:
                    last.then_inc(down_done, 1)

            g0 = GEMM_PIECES
            pe.wait_ge(tile_read, IN_TILES + KT)
            gemm2_by_k(g0, hlo_ready, {3: x_ssq})
            pe.wait_ge(rms_ready, KT + 3)
            gemm(g0 + 4, 0, 2)
            gemm(g0 + 6, 2, 3)

            def ffn_block(b, first, before_last=None):
                q, d = blk_q(b), (b - 1) * 16
                pe.wait_ge(*((z_ready, HEADS + 1) if first else (down_added, d)))
                gemm(q, 0, 0)
                pe.wait_ge(act_ready, b * 2)
                for j in range(16):
                    if j % 4 == 0:
                        pe.wait_ge(lo_ready, q + 3 + j // 4)
                    if j == 0:
                        pe.wait_ge(up_read, b * 2 - 1)
                    elif j == 1:
                        pe.wait_ge(z_ready, b * 2 + HEADS)
                    elif j == 2:
                        pe.wait_ge(up_read, b * 2)
                    elif j == 3:
                        pe.wait_ge(z_ready, b * 2 + (HEADS + 1))
                    else:
                        pe.wait_ge(down_added, d + (j - 3))
                    down_tile((2 + j // 4) % 4, j % 4, (j + 1) % 4)
                pe.wait_ge(down_added, d + 13)
                gemm(q + 6, 2, 1)
                pe.wait_ge(down_added, d + 14)
                gemm(q + 8, 0, 2)
                pe.wait_ge(down_added, d + 15)
                gemm(q + 10, 2, 3, q1=before_last)

            def states_t():
                pe.wait_ge(rows_saved, HEADS + FT)
                pe.wait_ge(up_read, FT - 1)
                pe.wait_ge(z_ready, HEADS + FT)
                for r in range(ROWS):
                    te.transpose(ps[0:FT, r // 4, (r % 4) * P:(r % 4 + 1) * P], ffn_rows[:, r, :], ident[:, :])
                te.transpose(ps[0:16, 4, 256:384], mix_rows[:, 0:2, :].rearrange("p r t -> p (r t)"), ident[:, :])
                te.transpose(ps[:, 4, 384:512], mix_rows[:, 2:, :].rearrange("p r t -> p (r t)"),
                             ident[:, :]).then_inc(rows_t, 1)

            ffn_block(1, True)
            with pe.Fori(2, NBLK - 1) as b:
                ffn_block(b, False)
            ffn_block(NBLK - 1, False, before_last=states_t)

            D0 = (NBLK - 1) * 16
            pe.wait_ge(lo_ready, blk_q(NBLK) + 1)
            pe.wait_ge(rows_staged, 1)
            pe.wait_ge(up_read, FT)
            for j in range(4):
                down_tile(0, j, j, ks=(0,))
            pe.wait_ge(act_ready, FT)
            for j in range(4):
                down_tile(0, j, j, ks=(1,))

            def out_t(j):
                s = j % 2
                pe.wait_ge(fg_ready, j + 1)
                if j >= 2:
                    pe.wait_ge(f_ready, j - 1)
                else:
                    pe.wait_ge(down_added, D0 + 4)
                for b in range(TB):
                    te.transpose(ps[:, 4 + 2 * s, b * P:(b + 1) * P], fin_g[s][:, b * P:(b + 1) * P], ident[:, :])
                te.transpose(ps[0:SAMP, 5 + 2 * s, 0:P], fin_g[s][:, SEQ:T], ident[:, :]).then_inc(f_t, 1)

            for j in range(4, 16):
                if j % 4 == 0:
                    pe.wait_ge(lo_ready, blk_q(NBLK) + j // 4 + 1)
                pe.wait_ge(down_added, D0 + (j - 1 if j >= 6 else j - 3))
                down_tile(j // 4, j % 4, j % 2)
                if j < 6:
                    out_t(2 * (j - 4))
                    out_t(2 * (j - 4) + 1)
                else:
                    out_t(j - 2)
            out_t(14)
            out_t(15)
            pe.wait_ge(facc_done, KT + 1)
            pe.wait_ge(down_added, D0 + 16)
            for tb in range(TB + 1):
                n = P if tb < TB else SAMP
                last = te.matmul(ps[0:n, 0, tb:tb + 1], acc[:, tb * P:tb * P + n], ones[:, 0:1], start=True, stop=True)
            last.then_inc(fssq_done, 1)


_INS = ["x_prompt", "x_sample", "state_conv_mix", "state_conv_ffn", "norm_mix_g", "w_in", "sgu_norm_g", "w_s",
        "b_s", "conv_mix_w", "conv_mix_b", "out_norm_a_g", "out_norm_b_g", "w_out", "norm_ffn_g", "w_gate",
        "w_up", "conv_ffn_w", "conv_ffn_b", "w_down", "final_norm_g"]
_OUTS = [(1, 512, 2048), (8, 8, 2048), (1, 1, 2, 1024), (1, 1, 2, 5632), (1, 8, 2, 1024), (1, 8, 2, 5632),
         (1, 8, 8, 1024)]


def kernel(**inputs):
    import numpy as _np
    import concourse.bacc as _bacc
    from concourse import mybir as _mybir
    from concourse.bass_utils import run_bass_kernel_spmd as _run

    nc = _bacc.Bacc("TRN2", target_bir_lowering=False, num_devices=1)
    arrays, args = {}, []
    for name in _INS:
        a = _np.ascontiguousarray(inputs[name])
        arrays[f"in_{name}_dram"] = a
        args.append(nc.dram_tensor(f"in_{name}_dram", a.shape, _mybir.dt.from_np(a.dtype), kind="ExternalInput").ap())
    for i, shape in enumerate(_OUTS):
        args.append(nc.dram_tensor(f"out_{i}_dram", shape, F32, kind="ExternalOutput").ap())
    build_layer(nc, *args)
    r = _run(nc, [arrays], core_ids=[0])
    return tuple(r.results[0][f"out_{i}_dram"] for i in range(len(_OUTS)))
```
